# Optimizing a Trainium2 kernel written in Bass

```python
import math
import jax, jax.numpy as jnp
from jax import lax
import numpy as np

D_MODEL = 1024
BATCH = 1
SEQ = 256
DEPTH = 2

N_A_LAYERS = DEPTH // 2
N_B_LAYERS = DEPTH - N_A_LAYERS
POOL_WINDOWS = (2, 4, 8, 16)
N_POOL_GROUPS = len(POOL_WINDOWS)
POOL_GROUP = D_MODEL // N_POOL_GROUPS
HEAD_DIM = 64
N_HEADS = D_MODEL // HEAD_DIM
MOBA_BLOCK = 256
MOBA_TOPK = 3
Q_BLOCK = 128
NUM_BUCKETS = 32
MAX_DISTANCE = 128
D_FF = -(-8 * D_MODEL // (3 * 256)) * 256
EPS = 1e-6


def rmsnorm(x, g):
    xf = x.astype(jnp.float32)
    y = xf * lax.rsqrt(jnp.mean(xf * xf, axis=-1, keepdims=True) + EPS)
    return (y * g.astype(jnp.float32)).astype(x.dtype)

def pool_mixer(h, w, scale):
    B, T, D = h.shape
    hf = h.astype(jnp.float32)
    csum = jnp.concatenate([jnp.zeros((B, 1, D), jnp.float32), jnp.cumsum(hf, axis=1)], axis=1)
    t = jnp.arange(T)
    outs = []
    for g, win in enumerate(POOL_WINDOWS):
        sl = slice(g * POOL_GROUP, (g + 1) * POOL_GROUP)
        start = jnp.maximum(t + 1 - win, 0)
        cnt = (t + 1 - start).astype(jnp.float32)
        window_sum = csum[:, 1:, sl] - jnp.take(csum[:, :, sl], start, axis=1)
        outs.append(window_sum / cnt[None, :, None] - hf[:, :, sl])
    d = jnp.stack(outs, axis=2).astype(h.dtype)
    y = jnp.einsum('btgc,gce->btge', d, w).reshape(B, T, D)
    return y * scale

def swiglu(h, w_gate_up, w_down):
    gu = h @ w_gate_up
    gate, up = jnp.split(gu, 2, axis=-1)
    return (jax.nn.silu(gate) * up) @ w_down

def rel_bucket(n):
    max_exact = NUM_BUCKETS // 2
    nf = jnp.maximum(n, max_exact).astype(jnp.float32)
    large = max_exact + (jnp.log(nf / max_exact) / math.log(MAX_DISTANCE / max_exact)
                         * (NUM_BUCKETS - max_exact)).astype(jnp.int32)
    large = jnp.minimum(large, NUM_BUCKETS - 1)
    return jnp.where(n < max_exact, n, large)

def shared_kv(x, g, w_kv):
    B, T, D = x.shape
    h = rmsnorm(x, g)
    kv = h @ w_kv
    k, v = jnp.split(kv, 2, axis=-1)
    n_blocks = -(-T // MOBA_BLOCK)
    pad = n_blocks * MOBA_BLOCK - T

    def to_blocks(a):
        a = a.reshape(B, T, N_HEADS, HEAD_DIM).transpose(0, 2, 1, 3)
        a = jnp.pad(a, ((0, 0), (0, 0), (0, pad), (0, 0)))
        return a.reshape(B, N_HEADS, n_blocks, MOBA_BLOCK, HEAD_DIM)

    k_blocks = to_blocks(k)
    v_blocks = to_blocks(v)
    k_mean = jnp.mean(k_blocks.astype(jnp.float32), axis=3).astype(k_blocks.dtype)
    return k_blocks, v_blocks, k_mean

def moba_attention(q, k_blocks, v_blocks, k_mean, rel_bias):
    B, T = q.shape[0], q.shape[1]
    n_q = T // Q_BLOCK
    n_blocks = k_blocks.shape[2]
    topk = min(MOBA_TOPK, n_blocks)
    scale = HEAD_DIM ** -0.5
    h_idx = jnp.arange(N_HEADS)[:, None, None]
    bias_t = rel_bias.T.astype(jnp.float32)
    q_blocks = q.transpose(0, 2, 1, 3).reshape(B, N_HEADS, n_q, Q_BLOCK, HEAD_DIM)
    q_blocks = q_blocks.transpose(0, 2, 1, 3, 4).reshape(B * n_q, N_HEADS, Q_BLOCK, HEAD_DIM)
    b_idx = jnp.repeat(jnp.arange(B), n_q)
    qb_idx = jnp.tile(jnp.arange(n_q), B)
    j_blk = jnp.arange(MOBA_BLOCK)

    def step(args):
        qblk, b, qb = args
        kb = k_blocks[b]
        vb = v_blocks[b]
        km = k_mean[b]
        qs = qb * Q_BLOCK
        own = qs // MOBA_BLOCK
        qpos = qs + jnp.arange(Q_BLOCK)
        gate = jnp.einsum('hqd,hnd->hqn', qblk, km).astype(jnp.float32)
        gate = jnp.where(jnp.arange(n_blocks)[None, None, :] < own, gate, -jnp.inf)
        _, sel = lax.top_k(gate, topk)
        sel_valid = jnp.arange(topk) < jnp.minimum(own, topk)
        k_sel = kb[h_idx, sel]
        v_sel = vb[h_idx, sel]
        s_sel = jnp.einsum('hqd,hqkjd->hqkj', qblk, k_sel).astype(jnp.float32) * scale
        kpos_sel = sel[..., None] * MOBA_BLOCK + j_blk
        k_own = lax.dynamic_index_in_dim(kb, own, axis=1, keepdims=False)
        v_own = lax.dynamic_index_in_dim(vb, own, axis=1, keepdims=False)
        s_own = jnp.einsum('hqd,hjd->hqj', qblk, k_own).astype(jnp.float32) * scale
        kpos_own = own * MOBA_BLOCK + j_blk
        L_sel = topk * MOBA_BLOCK
        s = jnp.concatenate([s_sel.reshape(N_HEADS, Q_BLOCK, L_sel), s_own], axis=-1)
        kpos = jnp.concatenate([kpos_sel.reshape(N_HEADS, Q_BLOCK, L_sel),
                                jnp.broadcast_to(kpos_own[None, None, :], (N_HEADS, Q_BLOCK, MOBA_BLOCK))], axis=-1)
        valid_sel = jnp.broadcast_to(sel_valid[None, None, :, None], (N_HEADS, Q_BLOCK, topk, MOBA_BLOCK)).reshape(N_HEADS, Q_BLOCK, L_sel)
        valid_own = jnp.broadcast_to(kpos_own[None, None, :] <= qpos[None, :, None], (N_HEADS, Q_BLOCK, MOBA_BLOCK))
        valid = jnp.concatenate([valid_sel, valid_own], axis=-1)
        bucket = rel_bucket(jnp.maximum(qpos[None, :, None] - kpos, 0))
        bias = bias_t[h_idx, bucket]
        s = jnp.where(valid, s + bias, -jnp.inf)
        p = jax.nn.softmax(s, axis=-1).astype(vb.dtype)
        p_sel = p[..., :L_sel].reshape(N_HEADS, Q_BLOCK, topk, MOBA_BLOCK)
        p_own = p[..., L_sel:]
        return (jnp.einsum('hqkj,hqkjd->hqd', p_sel, v_sel)
                + jnp.einsum('hqj,hjd->hqd', p_own, v_own))

    o = lax.map(step, (q_blocks, b_idx, qb_idx))
    o = o.reshape(B, n_q, N_HEADS, Q_BLOCK, HEAD_DIM).transpose(0, 1, 3, 2, 4)
    return o.reshape(B, T, D_MODEL)

def first_inputs(seed: int = 0) -> dict:
    key = jax.random.key(seed)
    ks = jax.random.split(key, 14)
    f32 = jnp.float32
    nrm = lambda k, shape: jax.random.normal(k, shape, f32)
    x = nrm(ks[0], (BATCH, SEQ, D_MODEL))
    norm_mixer = 1.0 + 0.05 * nrm(ks[1], (DEPTH, D_MODEL))
    norm_ffn = 1.0 + 0.05 * nrm(ks[2], (DEPTH, D_MODEL))
    pool_w = nrm(ks[3], (N_A_LAYERS, N_POOL_GROUPS, POOL_GROUP, POOL_GROUP)) * POOL_GROUP ** -0.5
    pool_scale = 1.0 + 0.05 * nrm(ks[4], (N_A_LAYERS, D_MODEL))
    kv_norm = 1.0 + 0.05 * nrm(ks[5], (D_MODEL,))
    w_kv = nrm(ks[6], (D_MODEL, 2 * D_MODEL)) * D_MODEL ** -0.5
    w_q = nrm(ks[7], (N_B_LAYERS, D_MODEL, D_MODEL)) * D_MODEL ** -0.5
    w_o = nrm(ks[8], (N_B_LAYERS, D_MODEL, D_MODEL)) * D_MODEL ** -0.5
    rel_bias = 0.5 * nrm(ks[9], (NUM_BUCKETS, N_HEADS))
    w_gate_up = nrm(ks[10], (DEPTH, D_MODEL, 2 * D_FF)) * D_MODEL ** -0.5
    w_down = nrm(ks[11], (DEPTH, D_FF, D_MODEL)) * D_FF ** -0.5
    final_norm = 1.0 + 0.05 * nrm(ks[12], (D_MODEL,))
    return {'x': x, 'norm_mixer': norm_mixer, 'norm_ffn': norm_ffn, 'pool_w': pool_w,
            'pool_scale': pool_scale, 'kv_norm': kv_norm, 'w_kv': w_kv, 'w_q': w_q, 'w_o': w_o,
            'rel_bias': rel_bias, 'w_gate_up': w_gate_up, 'w_down': w_down, 'final_norm': final_norm}

def first_block(x, norm_mixer, norm_ffn, pool_w, pool_scale, kv_norm, w_kv, w_q, w_o,
              rel_bias, w_gate_up, w_down, final_norm):
    B, T, D = x.shape
    k_blocks = v_blocks = k_mean = None
    for layer in range(DEPTH):
        if layer < N_A_LAYERS:
            x = x + pool_mixer(rmsnorm(x, norm_mixer[layer]), pool_w[layer], pool_scale[layer])
        else:
            j = layer - N_A_LAYERS
            if j == 0:
                k_blocks, v_blocks, k_mean = shared_kv(x, kv_norm, w_kv)
            h = rmsnorm(x, norm_mixer[layer])
            q = (h @ w_q[j]).reshape(B, T, N_HEADS, HEAD_DIM)
            o = moba_attention(q, k_blocks, v_blocks, k_mean, rel_bias)
            x = x + o @ w_o[j]
        x = x + swiglu(rmsnorm(x, norm_ffn[layer]), w_gate_up[layer], w_down[layer])
    return rmsnorm(x, final_norm)


N_MIXERS = 4
N_HEADS_GROUP = D_MODEL // (N_MIXERS * HEAD_DIM)
GROUP_WIDTH = N_HEADS_GROUP * HEAD_DIM
MIX_WIDTH = N_MIXERS * GROUP_WIDTH
Q_BLK = 128
GRID_W = 64
NA_ROWS = 8
NA_COLS = 16
DIFF_QK_DIM = HEAD_DIM // 2
DIL_PATTERNS = ((128, 1), (512, 4), (2048, 16))
MLA_Q_RANK = D_MODEL // 4
MLA_KV_RANK = D_MODEL // 8
MLA_NOPE = HEAD_DIM
MLA_ROPE = HEAD_DIM // 2
MLA_V = HEAD_DIM
ROPE_THETA = 10000.0
T5_BUCKETS = 32
T5_MAX_DIST = 1024
T5_HEADS = 2 * N_HEADS_GROUP
D_FF_2 = ((8 * D_MODEL + 3 * 256 - 1) // (3 * 256)) * 256
IN_WIDTH = 9 * GROUP_WIDTH + MLA_Q_RANK + MLA_KV_RANK + MLA_ROPE


def rms_norm(x, g):
    xf = x.astype(jnp.float32)
    y = xf * lax.rsqrt(jnp.mean(xf * xf, axis=-1, keepdims=True) + EPS)
    return (y * g.astype(jnp.float32)).astype(x.dtype)

def t5_bucket(rel):
    nb = T5_BUCKETS // 2
    max_exact = nb // 2
    side = jnp.where(rel > 0, nb, 0)
    n = jnp.abs(rel)
    large = max_exact + (jnp.log(jnp.maximum(n, 1).astype(jnp.float32) / max_exact)
                         / math.log(T5_MAX_DIST / max_exact) * (nb - max_exact)).astype(jnp.int32)
    large = jnp.minimum(large, nb - 1)
    return side + jnp.where(n < max_exact, n, large)

def rope_tables(pos):
    half = MLA_ROPE // 2
    inv_freq = ROPE_THETA ** (-jnp.arange(half, dtype=jnp.float32) / half)
    ang = pos.astype(jnp.float32)[:, None] * inv_freq[None, :]
    return jnp.cos(ang), jnp.sin(ang)

def apply_rope(x, cos, sin):
    half = x.shape[-1] // 2
    x1 = x[..., :half].astype(jnp.float32)
    x2 = x[..., half:].astype(jnp.float32)
    return jnp.concatenate([x1 * cos - x2 * sin, x1 * sin + x2 * cos], axis=-1).astype(x.dtype)

def neighborhood_attention(q, k, v, rpb):
    B, S, H, D = q.shape
    rows = S // GRID_W
    wr = min(NA_ROWS, rows)
    scale = D ** -0.5
    kg = k.reshape(B, rows, GRID_W, H, D)
    vg = v.reshape(B, rows, GRID_W, H, D)
    qg = q.reshape(B, rows, GRID_W, H, D).swapaxes(0, 1)
    col = jnp.arange(GRID_W)
    col_idx = jnp.clip(col - NA_COLS // 2, 0, GRID_W - NA_COLS)[:, None] + jnp.arange(NA_COLS)[None, :]
    col_bias_idx = col_idx - col[:, None] + NA_COLS - 1

    def one_row(args):
        q_row, r = args
        r0 = jnp.clip(r - wr // 2, 0, rows - wr)
        k_rows = lax.dynamic_slice_in_dim(kg, r0, wr, axis=1)
        v_rows = lax.dynamic_slice_in_dim(vg, r0, wr, axis=1)
        k_nb = k_rows[:, :, col_idx]
        v_nb = v_rows[:, :, col_idx]
        row_bias_idx = r0 + jnp.arange(wr) - r + NA_ROWS - 1
        bias = rpb[:, row_bias_idx[None, :, None], col_bias_idx[:, None, :]]
        s = jnp.einsum('bqhd,brqchd->bhqrc', q_row, k_nb).astype(jnp.float32) * scale + bias.astype(jnp.float32)
        p = jax.nn.softmax(s.reshape(B, H, GRID_W, wr * NA_COLS), axis=-1).reshape(s.shape)
        return jnp.einsum('bhqrc,brqchd->bqhd', p.astype(v.dtype), v_nb)

    out = lax.map(one_row, (qg, jnp.arange(rows)))
    return out.swapaxes(0, 1).reshape(B, S, H * D)

def diff_attention(q, k, v, lam, lam_init, subln_g, table):
    B, S, H, _, dk = q.shape
    nblk = S // Q_BLK
    scale = dk ** -0.5
    qb = q.reshape(B, nblk, Q_BLK, H, 2, dk).swapaxes(0, 1)
    kpos = jnp.arange(S)

    def one_block(args):
        q_blk, i = args
        qpos = i * Q_BLK + jnp.arange(Q_BLK)
        bias = table[t5_bucket(kpos[None, :] - qpos[:, None])].transpose(2, 0, 1).astype(jnp.float32)
        s = jnp.einsum('bqhcd,bkhcd->bchqk', q_blk, k).astype(jnp.float32) * scale + bias[None, None]
        p = jax.nn.softmax(s, axis=-1)
        a = p[:, 0] - lam * p[:, 1]
        return jnp.einsum('bhqk,bkhd->bqhd', a.astype(v.dtype), v)

    o = lax.map(one_block, (qb, jnp.arange(nblk))).swapaxes(0, 1).reshape(B, S, H, -1)
    o = rms_norm(o, subln_g) * (1.0 - lam_init)
    return o.reshape(B, S, -1)

def dilated_attention(q, k, v, table):
    B, S, H, D = q.shape
    nblk = S // Q_BLK
    scale = D ** -0.5
    qb = q.reshape(B, nblk, Q_BLK, H, D).swapaxes(0, 1)

    def one_block(args):
        q_blk, i = args
        qpos = i * Q_BLK + jnp.arange(Q_BLK)
        outs, lses = [], []
        for window, dil in DIL_PATTERNS:
            m = window // (2 * dil)
            offs = dil * jnp.arange(-m, m + 1)
            kpos = qpos[:, None] + offs[None, :]
            valid = (kpos >= 0) & (kpos < S)
            kidx = jnp.clip(kpos, 0, S - 1)
            k_g = k[:, kidx]
            v_g = v[:, kidx]
            bias = table[t5_bucket(offs)].T.astype(jnp.float32)
            s = jnp.einsum('bqhd,bqkhd->bhqk', q_blk, k_g).astype(jnp.float32) * scale + bias[None, :, None, :]
            s = jnp.where(valid[None, None], s, -jnp.inf)
            s_max = jnp.max(s, axis=-1, keepdims=True)
            e = jnp.exp(s - s_max)
            den = jnp.sum(e, axis=-1)
            o = jnp.einsum('bhqk,bqkhd->bqhd', e, v_g.astype(jnp.float32)) / den.transpose(0, 2, 1)[..., None]
            outs.append(o)
            lses.append(s_max[..., 0] + jnp.log(den))
        wts = jax.nn.softmax(jnp.stack(lses), axis=0)
        out = jnp.sum(jnp.stack(outs) * wts.transpose(0, 1, 3, 2)[..., None], axis=0)
        return out.astype(q.dtype)

    out = lax.map(one_block, (qb, jnp.arange(nblk)))
    return out.swapaxes(0, 1).reshape(B, S, H * D)

def mla_attention(q_nope, q_rope, k_nope, k_rope, v):
    B, S, H, _ = q_nope.shape
    nblk = S // Q_BLK
    scale = (MLA_NOPE + MLA_ROPE) ** -0.5

    def blocks(t):
        return t.reshape(B, nblk, Q_BLK, *t.shape[2:]).swapaxes(0, 1)

    def one_block(args):
        qn, qr = args
        s = jnp.einsum('bqhd,bkhd->bhqk', qn, k_nope) + jnp.einsum('bqhd,bkd->bhqk', qr, k_rope)
        p = jax.nn.softmax(s.astype(jnp.float32) * scale, axis=-1)
        return jnp.einsum('bhqk,bkhd->bqhd', p.astype(v.dtype), v)

    out = lax.map(one_block, (blocks(q_nope), blocks(q_rope)))
    return out.swapaxes(0, 1).reshape(B, S, -1)

def second_inputs(seed: int = 0) -> dict:
    key = jax.random.key(seed)
    ks = jax.random.split(key, 17)
    H = N_HEADS_GROUP

    def nrm(k, shape, scale):
        return jax.random.normal(k, shape, jnp.float32) * scale

    return {
        'x': nrm(ks[0], (BATCH, SEQ, D_MODEL), 1.0),
        'attn_norm': 1.0 + nrm(ks[1], (DEPTH, D_MODEL), 0.05),
        'w_in': nrm(ks[2], (DEPTH, D_MODEL, IN_WIDTH), D_MODEL ** -0.5),
        'na_rpb': nrm(ks[3], (DEPTH, H, 2 * NA_ROWS - 1, 2 * NA_COLS - 1), 0.1),
        'diff_lambda': nrm(ks[4], (DEPTH, 4, DIFF_QK_DIM), 0.1),
        'diff_subln': 1.0 + nrm(ks[5], (DEPTH, HEAD_DIM), 0.05),
        'mla_q_norm': 1.0 + nrm(ks[6], (DEPTH, MLA_Q_RANK), 0.05),
        'w_uq': nrm(ks[7], (DEPTH, MLA_Q_RANK, H * (MLA_NOPE + MLA_ROPE)), MLA_Q_RANK ** -0.5),
        'mla_kv_norm': 1.0 + nrm(ks[8], (DEPTH, MLA_KV_RANK), 0.05),
        'w_ukv': nrm(ks[9], (DEPTH, MLA_KV_RANK, H * (MLA_NOPE + MLA_V)), MLA_KV_RANK ** -0.5),
        't5_table': nrm(ks[10], (T5_BUCKETS, T5_HEADS), 0.1),
        'w_o': nrm(ks[11], (DEPTH, MIX_WIDTH, D_MODEL), MIX_WIDTH ** -0.5),
        'ffn_norm': 1.0 + nrm(ks[12], (DEPTH, D_MODEL), 0.05),
        'w_gate': nrm(ks[13], (DEPTH, D_MODEL, D_FF_2), D_MODEL ** -0.5),
        'w_up': nrm(ks[14], (DEPTH, D_MODEL, D_FF_2), D_MODEL ** -0.5),
        'w_down': nrm(ks[15], (DEPTH, D_FF_2, D_MODEL), D_FF_2 ** -0.5),
        'final_norm': 1.0 + nrm(ks[16], (D_MODEL,), 0.05),
    }

def second_block(x, attn_norm, w_in, na_rpb, diff_lambda, diff_subln, mla_q_norm, w_uq,
              mla_kv_norm, w_ukv, t5_table, w_o, ffn_norm, w_gate, w_up, w_down, final_norm):
    B, S, _ = x.shape
    H, G = N_HEADS_GROUP, GROUP_WIDTH
    cos, sin = rope_tables(jnp.arange(S))
    t5_diff = t5_table[:, :H]
    t5_dil = t5_table[:, H:]
    split_points = np.cumsum([G] * 9 + [MLA_Q_RANK, MLA_KV_RANK]).tolist()
    for l in range(DEPTH):
        h = rms_norm(x, attn_norm[l])
        proj = h @ w_in[l]
        qa, ka, va, qb, kb, vb, qc, kc, vc, cq, ckv, kr = jnp.split(proj, split_points, axis=-1)

        o_a = neighborhood_attention(qa.reshape(B, S, H, HEAD_DIM), ka.reshape(B, S, H, HEAD_DIM),
                                     va.reshape(B, S, H, HEAD_DIM), na_rpb[l])

        lam_init = 0.8 - 0.6 * math.exp(-0.3 * l)
        lq1, lk1, lq2, lk2 = [diff_lambda[l, j].astype(jnp.float32) for j in range(4)]
        lam = jnp.exp(jnp.sum(lq1 * lk1)) - jnp.exp(jnp.sum(lq2 * lk2)) + lam_init
        o_b = diff_attention(qb.reshape(B, S, H, 2, DIFF_QK_DIM), kb.reshape(B, S, H, 2, DIFF_QK_DIM),
                             vb.reshape(B, S, H, HEAD_DIM), lam, lam_init, diff_subln[l], t5_diff)

        o_c = dilated_attention(qc.reshape(B, S, H, HEAD_DIM), kc.reshape(B, S, H, HEAD_DIM),
                                vc.reshape(B, S, H, HEAD_DIM), t5_dil)

        cq = rms_norm(cq, mla_q_norm[l])
        qd = (cq @ w_uq[l]).reshape(B, S, H, MLA_NOPE + MLA_ROPE)
        q_nope = qd[..., :MLA_NOPE]
        q_rope = apply_rope(qd[..., MLA_NOPE:], cos[:, None, :], sin[:, None, :])
        ckv = rms_norm(ckv, mla_kv_norm[l])
        kvd = (ckv @ w_ukv[l]).reshape(B, S, H, MLA_NOPE + MLA_V)
        k_nope = kvd[..., :MLA_NOPE]
        v_d = kvd[..., MLA_NOPE:]
        k_rope = apply_rope(kr, cos, sin)
        o_d = mla_attention(q_nope, q_rope, k_nope, k_rope, v_d)

        mix = jnp.concatenate([o_a, o_b, o_c, o_d], axis=-1)
        x = x + mix @ w_o[l]

        h = rms_norm(x, ffn_norm[l])
        x = x + (jax.nn.silu(h @ w_gate[l]) * (h @ w_up[l])) @ w_down[l]
    return rms_norm(x, final_norm)


def setup_inputs(seed=0):
    out = dict(first_inputs(seed))
    for name, value in second_inputs(seed + 1).items():
        if name != "x":
            out[name + "_2"] = value
    return out


def reference(
    x, norm_mixer, norm_ffn, pool_w, pool_scale, kv_norm, w_kv, w_q, w_o, rel_bias, w_gate_up,
    w_down, final_norm, attn_norm_2, w_in_2, na_rpb_2, diff_lambda_2, diff_subln_2,
    mla_q_norm_2, w_uq_2, mla_kv_norm_2, w_ukv_2, t5_table_2, w_o_2, ffn_norm_2, w_gate_2,
    w_up_2, w_down_2, final_norm_2,
):
    x = first_block(
        x, norm_mixer, norm_ffn, pool_w, pool_scale, kv_norm, w_kv, w_q, w_o, rel_bias,
        w_gate_up, w_down, final_norm,
    )
    return second_block(
        x, attn_norm_2, w_in_2, na_rpb_2, diff_lambda_2, diff_subln_2, mla_q_norm_2, w_uq_2,
        mla_kv_norm_2, w_ukv_2, t5_table_2, w_o_2, ffn_norm_2, w_gate_2, w_up_2, w_down_2,
        final_norm_2,
    )


_drawn_inputs = setup_inputs


def setup_inputs(seed=0):
    import zlib

    import numpy as np

    out = dict(_drawn_inputs(seed))
    spreads = {}
    factors = {'kv_norm': 2.668, 'na_rpb_2': 4.45, 'mla_q_norm_2': 8.0, 'mla_kv_norm_2': 6.864}
    for name, (base, spread) in spreads.items():
        noise = np.random.default_rng([zlib.crc32(name.encode()), seed]).standard_normal(out[name].shape)
        drawn = base * np.exp(spread * noise) if base else spread * noise
        out[name] = __import__('jax').numpy.asarray(drawn.astype(out[name].dtype))
    for name, factor in factors.items():
        out[name] = (out[name] * factor).astype(out[name].dtype)
    return out
```

```python
import math
from contextlib import ExitStack

import numpy as np

import concourse.bass as bass
from concourse import mybir

F32 = mybir.dt.float32
F32R = mybir.dt.float32r
ALU = mybir.AluOpType
ACT = mybir.ActivationFunctionType
AX_X = mybir.AxisListType.X

P = 128
T = 256
D = 1024
TT = T // P
KC = D // P
HALF = 512
DFF = 2816
FB = 256
NB = DFF // FB
FFN_UNITS = 3 * NB
UNIT = 2048
SLOTS = 3
EPS = 1e-6
NEG = -1e30
BIG = 3.0e38
HD = 64
NBUCKET = 32
SEQ_D = 2 * T
MLA_QR, MLA_KVR, ROPE = 256, 128, 32
MLA_D = HD + ROPE
IN_W = 2720

POOL_U = 0
FFN_U = [1, 50, 98, 146]
MOBA_U = 34
MIX_U = [83, 131]
N_UNITS = 179


def _bucket_moba(n):
    exact = NBUCKET // 2
    nf = np.maximum(n, exact).astype(np.float32)
    large = exact + (np.log(nf / np.float32(exact)) / np.float32(math.log(128 / exact))
                     * np.float32(NBUCKET - exact)).astype(np.int32)
    return np.where(n < exact, n, np.minimum(large, NBUCKET - 1))


def _bucket_t5(rel):
    nb = NBUCKET // 2
    exact = nb // 2
    n = np.abs(rel)
    large = exact + (np.log(np.maximum(n, 1).astype(np.float32) / np.float32(exact))
                     / np.float32(math.log(1024 / exact)) * np.float32(nb - exact)).astype(np.int32)
    return np.where(rel > 0, nb, 0) + np.where(n < exact, n, np.minimum(large, nb - 1))


def shape_constants():
    f = np.float32
    out = {}
    out["c_ident"] = np.eye(P, dtype=f)
    t = np.arange(T)
    band = np.zeros((4, T, T), f)
    for g, win in enumerate((2, 4, 8, 16)):
        start = np.maximum(t + 1 - win, 0)
        s = t[:, None]
        inside = (s <= t[None, :]) & (s >= start[None, :])
        band[g] = np.where(inside, (f(1) / (t + 1 - start).astype(f))[None, :], f(0)) - np.eye(T, dtype=f)
    out["c_band"] = band
    d = np.arange(-(T - 1), T)
    moba = np.zeros((NBUCKET + 1, SEQ_D), f)
    past = d <= 0
    moba[_bucket_moba(np.maximum(-d, 0))[past], np.arange(d.size)[past]] = 1
    moba[NBUCKET, :d.size] = np.where(past, 0, NEG)
    moba[:, :d.size] = moba[:, :d.size][:, ::-1].copy()
    out["c_moba"] = moba
    t5 = np.zeros((2, NBUCKET + 1, SEQ_D), f)
    t5[:, _bucket_t5(d), np.arange(d.size)] = 1
    count = sum(((np.abs(d) <= (w // (2 * r)) * r) & (d % r == 0)).astype(int)
                for w, r in ((128, 1), (512, 4), (2048, 16)))
    t5[1, NBUCKET, :d.size] = np.where(count > 0, np.log(np.maximum(count, 1)), NEG)
    t5[:, :, :d.size] = t5[:, :, :d.size][:, :, ::-1].copy()
    out["c_t5"] = t5
    c = np.arange(64)
    first = np.clip(c - 8, 0, 48)[:, None]
    inside = (c[None, :] >= first) & (c[None, :] < first + 16)
    out["c_nmask"] = np.tile(np.where(inside, 0, NEG).astype(f)[:, ::-1], (2, 1))
    half = ROPE // 2
    inv = f(10000.0) ** (-np.arange(half, dtype=f) / f(half))
    ang = t.astype(f)[:, None] * inv[None, :]
    cos, sin = np.cos(ang).T, np.sin(ang).T
    k = np.concatenate([cos, cos, -sin, sin]).astype(f)
    out["c_rope"] = np.stack([(k * f(MLA_D ** -0.5)).astype(f), k], axis=1)
    return out


def moba_script():
    s = [("q_norm",)]
    def unit(n):
        return [("unit", n), ("split", n + 2), ("proj", n)]
    s += unit(0) + [("kv_norm",)]
    for n in range(1, 6):
        s += unit(n)
    def S(*x):
        return [("S", i) for i in x] + [("N", i) for i in x]
    def TH(*x):
        return [("T", i) for i in x]
    for g in range(4):
        i = 4 * g
        s += S(i, i + 1) + unit(6 + 2 * g)
        s += TH(i) + S(i + 2, i + 3) + TH(i + 1) + unit(7 + 2 * g)
        s += TH(i + 2, i + 3) + [("V", i + h) for h in range(4)] + [("O", g)]
    s += unit(14) + [("unit", 15), ("split", 17)]
    return s


def mix_script():
    s = []
    def unit(n):
        return [("unit", n), ("split", n + 2), ("proj", n)]
    def S(*x):
        return [("S", i) for i in x]
    def N(*x):
        return [("N", i) for i in x]
    def TH(*x):
        return [("T", i) for i in x]
    def V(*x):
        return [("V", i) for i in x]
    s += unit(0) + unit(1) + unit(2) + [("mla_T",)] + unit(3) + [("mla_G",)] + unit(4)
    s += S(0, 1) + N(0, 1) + unit(5)
    s += TH(0) + S(2, 3) + N(2, 3) + TH(1) + unit(6)
    s += S(4, 5) + N(4, 5) + TH(2, 3) + V(0, 1, 2, 3) + [("O", 0)] + S(6, 7) + N(6, 7) + unit(7)
    s += TH(4) + S(8, 9) + N(8, 9) + TH(5) + unit(8)
    s += S(10, 11) + N(10, 11) + TH(6, 7) + V(4, 5, 6, 7) + [("O", 1)] + S(12, 13) + N(12, 13) + unit(9)
    s += S(14, 15) + N(14, 15) + TH(8, 9, 10, 11) + V(8, 9, 10, 11) + [("diff_stats",)] + unit(10)
    s += [("diff_norm",)] + S(16, 17) + N(16, 17) + [("diff_T",)] + unit(11)
    s += TH(12) + S(18, 19) + N(18, 19) + TH(13) + unit(12)
    s += TH(14, 15) + V(12, 13, 14, 15) + [("O", 3)] + unit(13) + [("unit", 14), ("split", 16)]
    return s


def bass_two_stacks(nc, a, c, out):
    ctx = ExitStack()
    with ctx:
        def sb(name, shape, dt=F32):
            return ctx.enter_context(nc.sbuf_tensor(name, shape, dt))

        def sem(name):
            return ctx.enter_context(nc.semaphore(name))

        raw = sb("raw", [P, SLOTS, UNIT])
        whi = sb("whi", [P, SLOTS, UNIT], F32R)
        wlo = sb("wlo", [P, SLOTS, UNIT], F32R)
        x = sb("x", [P, TT, D])
        xn = sb("xn", [P, TT, D])
        gains = sb("gains", [P, 2, D])
        h_hi = sb("h_hi", [P, KC, T], F32R)
        h_lo = sb("h_lo", [P, KC, T], F32R)
        o_hi = sb("o_hi", [P, KC, T], F32R)
        o_lo = sb("o_lo", [P, KC, T], F32R)
        qall = sb("qall", [P, KC, T])
        qg = sb("qg", [P, 2, 2, T])
        kg = sb("kg", [P, 2, 2, T])
        vg = sb("vg", [P, 2, TT, 4 * HD])
        bias = sb("bias", [P, 5120])
        pr = sb("pr", [P, 8, 2, T])
        pt = sb("pt", [P, 4, 2 * T])
        ident = sb("ident", [P, P])
        junk = sb("junk", [P, HALF], mybir.dt.bfloat16)
        ssq = sb("ssq", [P, TT, 2])
        msq = sb("msq", [P, 8])
        rstd = sb("rstd", [P, 8])
        neghalf = sb("neghalf", [P, 8])
        negmax = sb("negmax", [P, 8, 2])
        psumrow = sb("psumrow", [P, 8, 2])
        rsum = sb("rsum", [P, 8, 2])
        dsq = sb("dsq", [P, 8])
        dms = sb("dms", [P, 8])
        drs = sb("drs", [P, 8])
        msm = sb("msm", [P, 4])
        tab_moba = sb("tab_moba", [NBUCKET + 1, 16])
        tab_t5 = sb("tab_t5", [NBUCKET + 1, 8])
        nmask = sb("nmask", [P, 64])
        rope = sb("rope", [P, 2, T])
        lam_in = sb("lam_in", [P, 2, P])
        lam_s = sb("lam_s", [P, 2, 2])
        lam_e = sb("lam_e", [P, 2, 2])
        neglam = sb("neglam", [P, 2])
        subln = sb("subln", [P, 2])
        subln_s = sb("subln_s", [P, 2])
        mlag = sb("mlag", [P, 2, 3])
        wuq = sb("wuq", [P, 2, 4, P])
        wukv = sb("wukv", [P, 4, 2, HD])

        band = qall[:, :, :].rearrange("p (g s) t -> p g s t", g=4)
        vecs = pr[:, 0:3, :, :].rearrange("p i a b -> p i (a b)")
        onehots = pr[:, 3:6, :, :].rearrange("p i a b -> p i (a b)")
        rpb_pad = pr[:, 6, 0, 0:P]
        sil = pr[:, 0, :, :].rearrange("p a b -> p (a b)")
        act32 = pr[:, 1, :, :].rearrange("p a b -> p (a b)")
        def latq(t):
            return xn[:, 0, t * MLA_QR:(t + 1) * MLA_QR]

        def latkv(t):
            return xn[:, 0, 2 * MLA_QR + t * MLA_KVR:2 * MLA_QR + (t + 1) * MLA_KVR]

        latT = xn[:, 1, 0:768].rearrange("p (c t) -> p c t", c=3)
        ropet = pt[:, 2:4, :]
        dno = xn[:, 0, 0:HALF]
        dsquare = xn[:, 0, HALF:D]
        bias_moba = bias[:, 0:16 * T].rearrange("p (h k) -> p h k", h=16)
        bias_diff = bias[:, 0:4 * 384].rearrange("p (h k) -> p h k", h=4)
        bias_dil = bias[:, 1536:3072].rearrange("p (h k) -> p h k", h=4)
        bias_na = bias[:, 3072:5120].rearrange("p (q h k) -> p q h k", q=2, h=4)

        bank = [ctx.enter_context(nc.psum_tensor(f"bank{i}", [P, HALF], F32)) for i in range(8)]
        ACC = [4, 5, 6, 7]

        vec_dram = nc.dram_tensor("vec_scratch", [24, SEQ_D], F32, kind="Internal")
        rpb_dram = nc.dram_tensor("rpb_scratch", [120, P], F32, kind="Internal")

        raw_in = [sem(f"raw_in{i}") for i in range(SLOTS)]
        hi_ready, lo_ready, units_used = sem("hi_ready"), sem("lo_ready"), sem("units_used")
        x_in = sem("x_in")
        small_in = sem("small_in")
        table_in, onehot_in = sem("table_in"), sem("onehot_in")
        layer_in = [sem("layer_in0"), sem("layer_in1")]
        gains_in = [sem("gains_in0"), sem("gains_in1")]
        band_in = sem("band_in")
        scratch_out, bias_in, bias2_in, na_in = sem("scratch_out"), sem("bias_in"), sem("bias2_in"), sem("na_in")
        na_ready = sem("na_ready")
        consts_set, pad_set, vec_done, vec_out = sem("consts_set"), sem("pad_set"), sem("vec_done"), sem("vec_out")
        x_ready, squares, msq_ready, rstd_ready = sem("x_ready"), sem("squares"), sem("msq_ready"), sem("rstd_ready")
        xn_ready, xT_ready, hT_hi, hT_lo = sem("xn_ready"), sem("xT_ready"), sem("hT_hi"), sem("hT_lo")
        acc_ready = sem("acc_ready")
        silu_ready, glu_ready, act_hi, act_ready = sem("silu_ready"), sem("glu_ready"), sem("act_hi"), sem("act_ready")
        proj_out = sem("proj_out")
        scores, maxed, exped, summed, normed = sem("scores"), sem("maxed"), sem("exped"), sem("summed"), sem("normed")
        transposed, pt_ready, pv_done = sem("transposed"), sem("pt_ready"), sem("pv_done")
        out_hi, out_lo = sem("out_hi"), sem("out_lo")
        mla_sq, mla_ms, mla_rs, mla_lat, mla_t, mla_tT = (sem("mla_sq"), sem("mla_ms"), sem("mla_rs"),
                                                          sem("mla_lat"), sem("mla_t"), sem("mla_tT"))
        mla_g, mla_rope, mla_qk, mla_copied = sem("mla_g"), sem("mla_rope"), sem("mla_qk"), sem("mla_copied")
        d_sq, d_red, d_ms, d_rs, d_n = sem("d_sq"), sem("d_red"), sem("d_ms"), sem("d_rs"), sem("d_n")
        lam_r, lam_x, lam_done, vchain = sem("lam_r"), sem("lam_x"), sem("lam_done"), sem("vchain")
        pool_d, rpb_in, ones_set = sem("pool_d"), sem("rpb_in"), sem("ones_set")
        fin, stored = sem("fin"), sem("stored")

        NORM_X = {0: 0, 1: 1, 2: 2, 3: 2, 4: 3, 5: 4, 6: 5, 7: 6, 8: 7, 9: 8, 10: 9}
        XN_NO = {0: 0, 1: 1, 2: 2, 3: 3, 4: 4, 6: 5, 7: 6, 8: 7, 9: 8}
        HT_NO = {0: 0, 1: 1, 2: 2, 3: 3, 4: 4, 6: 5, 7: 6, 8: 7, 9: 8}
        ACC_NO = {1: 0, 2: 1, 3: 2, 4: 3, 6: 4, 7: 5, 8: 6, 9: 7}
        GAIN_SRC = {0: a["norm_mixer"][0], 1: a["norm_ffn"][0], 2: a["norm_mixer"][1], 3: a["kv_norm"],
                    4: a["norm_ffn"][1], 5: a["final_norm"], 6: a["attn_norm_2"][0], 7: a["ffn_norm_2"][0],
                    8: a["attn_norm_2"][1], 9: a["ffn_norm_2"][1], 10: a["final_norm_2"]}

        LAST_U = {1: POOL_U, 2: FFN_U[0] + 32, 3: MOBA_U + 15, 4: FFN_U[1] + 32, 6: MIX_U[0] + 14,
                  7: FFN_U[2] + 32, 8: MIX_U[1] + 14, 9: FFN_U[3] + 32}
        OUT_HI = [{0: 4, 1: 5, 3: 6}, {0: 7, 1: 8, 3: 9}]
        OUT_LO = [[4, 5, 6, 7], [8, 9, 10, 11]]
        T_DIFF = 12

        def stage_items(layer):
            return 16 + 20 * layer, 16 + 17 * layer, 12 + 9 * layer

        def item_of_head(h):
            return h if h < 8 else 8 + 2 * (h - 8) if h < 12 else h + 4

        T_BEFORE = {}
        freed = {i: i + 1 for i in range(16)}
        for l in range(2):
            i0, q0, _ = stage_items(l)
            nt = 0
            for ev in mix_script():
                if ev[0] == "T":
                    first = item_of_head(ev[1])
                    for i in range(first, first + (2 if 8 <= ev[1] < 12 else 1)):
                        freed[i0 + i] = q0 + nt + 1
                if ev[0] in ("T", "diff_T"):
                    nt += 1
        for i in range(8, 56):
            T_BEFORE[i] = freed[i - 8]

        def down_from(tile, start, n):
            ap = tile[:, 0:n]
            return bass.AP(ap.tensor, ap.offset + start, [list(ap.ap[0]), [-1, n]])

        def kr_parts(dst, src):
            d = dst[:, 0:KC * 192].rearrange("p (k n) -> p k n", k=KC)
            s = src[:, 0:KC * 160].rearrange("p (k n) -> p k n", k=KC)
            return [(d[:, :, 0:160], s[:, :, 0:160]), (d[:, :, 160:176], s[:, :, 144:160]),
                    (d[:, :, 176:192], s[:, :, 128:144])]

        def slot_of(n):
            return n % SLOTS

        def k8(w, c0, width=FB):
            return w[:, bass.ds(c0, width)].rearrange("(k p) n -> p k n", p=P)

        def k2(w, r0):
            return w[bass.ds(r0, 2 * P), :].rearrange("(k p) n -> p k n", p=P)

        def ffn_weights(f):
            if f < 2:
                gu = a["w_gate_up"][f]
                return gu[:, 0:DFF], gu[:, DFF:2 * DFF], a["w_down"][f]
            return a["w_gate_2"][f - 2], a["w_up_2"][f - 2], a["w_down_2"][f - 2]

        W_IN_COLS = [2304, 2560, 256, 0, 512, 1024, 768, 1280, 1792, 1536, 2048]
        MIX_O_ROWS = [768, 0, 256, 512]
        MIX_OUT_CHUNK = [6, 0, 2, 4]

        def moba_src(n):
            if n < 4:
                return k8(a["w_q"][0], 256 * n)
            if n < 12:
                g = (n - 4) // 2
                return k8(a["w_kv"], 256 * g + (D if n % 2 else 0))
            return k2(a["w_o"][0], 256 * (n - 12))

        def mix_src(layer, n):
            if n == 1:
                return k8(a["w_in_2"][layer], 2560, 160)
            if n < 11:
                return k8(a["w_in_2"][layer], W_IN_COLS[n])
            return k2(a["w_o_2"][layer], MIX_O_ROWS[n - 11])

        block = ctx.enter_context(nc.Block())

        @block.sync
        def _(sp):
            def load(src, n, b=0, slot=None):
                if not (isinstance(n, int) and n < SLOTS and isinstance(b, int)):
                    sp.wait_ge(lo_ready, n - 2 + 3 * b)
                s = slot_of(n)
                dst = raw[:, s, :]
                if tuple(src.shape)[1:] == (KC, 160):
                    dst = raw[:, s, 0:KC * 160]
                dst = dst.rearrange("p (k n) -> p k n", k=src.shape[1])
                sp.dma_start(dst, src).then_inc(raw_in[s], 16)

            def load_gain(j):
                if j >= 2:
                    prev = j - 2
                    if prev == 5:
                        sp.wait_ge(x_ready, 4 * 5)
                    else:
                        sp.wait_ge(xn_ready, 4 * XN_NO[prev] + 4)
                sp.dma_start(gains[:, j % 2, :], GAIN_SRC[j].unsqueeze(0).broadcast_to([P, D])).then_inc(gains_in[j % 2], 16)

            xv = a["x"].rearrange("a (t p) d -> (a t) p d", p=P)
            for t in range(TT):
                sp.dma_start(x[:, t, :], xv[t]).then_inc(x_in, 16)
            load_gain(0)
            sp.dma_start(band, c["c_band"].rearrange("g (s p) t -> p g s t", p=P)).then_inc(band_in, 16)
            sp.dma_start(raw[:, 0, :].rearrange("p (g k n) -> p (g k) n", g=4, k=2),
                         a["pool_w"].rearrange("a g (k p) n -> p (a g k) n", p=P)).then_inc(raw_in[0], 16)
            sp.dma_start(pt[:, 0:2, :].rearrange("p a b -> p (a b)"), a["pool_scale"].broadcast_to([P, D])).then_inc(small_in, 16)
            sp.dma_start(ident[:, :], c["c_ident"]).then_inc(small_in, 16)
            load_gain(1)
            sp.dma_start(tab_moba[0:NBUCKET, :], a["rel_bias"]).then_inc(table_in, 16)
            sp.dma_start(tab_t5[0:NBUCKET, :], a["t5_table_2"]).then_inc(table_in, 16)
            sp.dma_start(onehots[0:NBUCKET + 1, 0, :], c["c_moba"]).then_inc(onehot_in, 16)
            for i in range(2):
                sp.dma_start(onehots[0:NBUCKET + 1, 1 + i, :], c["c_t5"][i]).then_inc(onehot_in, 16)
            sp.dma_start(nmask[:, :], c["c_nmask"]).then_inc(small_in, 16)
            sp.dma_start(rope[64:128, :, :], c["c_rope"]).then_inc(small_in, 16)
            for l in range(2):
                lam = a["diff_lambda_2"][l].rearrange("a b -> (a b)")
                sp.dma_start(lam_in[:, l, :], lam.unsqueeze(0).broadcast_to([P, P])).then_inc(small_in, 16)
                for r in range(2):
                    sp.dma_start(subln[64 * r:64 * r + 64, l:l + 1], a["diff_subln_2"][l].unsqueeze(1)).then_inc(small_in, 16)
                for k in range(2):
                    sp.dma_start(mlag[:, l, k:k + 1], a["mla_q_norm_2"][l, k * P:(k + 1) * P].unsqueeze(1)).then_inc(small_in, 16)
                sp.dma_start(mlag[:, l, 2:3], a["mla_kv_norm_2"][l].unsqueeze(1)).then_inc(small_in, 16)
            sp.wait_ge(pad_set, 1)
            sp.dma_start(rpb_pad[0:120, 48:79], a["na_rpb_2"].rearrange("l h r c -> (l h r) c")).then_inc(rpb_in, 16)

            def load_layer(l):
                if l:
                    sp.wait_ge(mla_g, 3)
                u = a["w_uq_2"][l].rearrange("(k p) (h n) -> p k h n", p=P, h=4)
                for k in range(2):
                    for lo, hi, at in ((0, MLA_D, 0), (80, 96, 96), (64, 80, 112)):
                        sp.dma_start(wuq[:, k, :, at:at + hi - lo], u[:, k, :, lo:hi]).then_inc(layer_in[l], 16)
                sp.dma_start(wukv[:, :, :, :].rearrange("p h a n -> p (h a n)"), a["w_ukv_2"][l]).then_inc(layer_in[l], 16)

            def ffn(f):
                u0 = FFN_U[f]
                wg, wu, wd = ffn_weights(f)
                load(k8(wg, 0), u0)
                load(k8(wu, 0), u0 + 1)
                load(k8(wg, FB), u0 + 2)
                load(k8(wu, FB), u0 + 3)
                load(k2(wd, 0), u0 + 4)
                yield
                with sp.Fori(2, NB - 1) as b:
                    load(k8(wg, b * FB), u0 - 1, b)
                    load(k8(wu, b * FB), u0, b)
                    load(k2(wd, (b - 1) * FB), u0 + 1, b)
                n = u0 + 3 * (NB - 1)
                load(k8(wg, (NB - 1) * FB), n - 1)
                load(k8(wu, (NB - 1) * FB), n)
                load(k2(wd, (NB - 2) * FB), n + 1)
                load(k2(wd, (NB - 1) * FB), n + 2)
                yield

            stage = ffn(0)
            next(stage)
            load_gain(2)
            load_gain(3)
            sp.wait_ge(vec_out, 3)
            for r0, nr, i in ((0, 16, 0), (16, 4, 1), (20, 4, 2)):
                sp.dma_start(vec_dram.ap()[r0:r0 + nr, :], vecs[0:nr, i, :]).then_inc(scratch_out, 16)
            sp.wait_ge(rpb_in, 16)
            sp.dma_start(rpb_dram.ap(), rpb_pad[0:120, :]).then_inc(scratch_out, 16)
            sp.wait_ge(scratch_out, 64)
            sp.dma_start(bias_moba, bass.AP(vec_dram, P, [[1, P], [SEQ_D, 16], [1, T]])).then_inc(bias_in, 16)
            load_layer(0)
            next(stage)

            for n in range(16):
                load(moba_src(n), MOBA_U + n)
                if n == 5:
                    load_gain(4)
                    load_gain(5)

            def load_na(l):
                for r in range(4):
                    for h in range(4):
                        off = ((l * 4 + h) * 15 + 4 + r) * P
                        sp.dma_start(bias_na[64 * (r % 2):64 * (r % 2) + 64, r // 2, h, :].rearrange("p (a b) -> p a b", a=4),
                                     bass.AP(rpb_dram, off, [[1, 64], [P, 4], [1, 64]])).then_inc(na_in, 16)

            stage = ffn(1)
            next(stage)
            sp.wait_ge(normed, 16)
            for i, dst in ((0, bias_diff), (1, bias_dil)):
                sp.dma_start(dst, bass.AP(vec_dram, (16 + 4 * i) * SEQ_D, [[1, P], [SEQ_D, 4], [1, 384]])).then_inc(bias2_in, 16)
            load_na(0)
            load_gain(6)
            next(stage)
            for l in range(2):
                for n in range(15):
                    load(mix_src(l, n), MIX_U[l] + n)
                    if n == 3:
                        load_gain(7 if l == 0 else 10)
                        if l == 0:
                            load_gain(8)
                if l == 0:
                    stage = ffn(2)
                    next(stage)
                    load_gain(9)
                    load_layer(1)
                    sp.wait_ge(exped, 16 + 8)
                    load_na(1)
                    next(stage)
            stage = ffn(3)
            next(stage)
            next(stage)
            ov = out.rearrange("a (t p) d -> (a t) p d", p=P)
            for t in range(TT):
                for h in range(2):
                    sp.wait_ge(fin, 2 * t + h + 1)
                    sp.dma_start(ov[t][:, h * HALF:(h + 1) * HALF], xn[:, t, h * HALF:(h + 1) * HALF]).then_inc(stored, 16)
            sp.wait_ge(stored, 64)

        @block.gpsimd
        def _(pool):
            pool.memset(neghalf[:, :], -0.5).then_inc(consts_set, 1)
            pool.wait_ge(consts_set, 1)
            pool.memset(rpb_pad, 0.0).then_inc(pad_set, 1)

            def rsqrt(version):
                for t in range(TT):
                    pool.wait_ge(msq_ready, 2 * version + t + 1)
                    pool.tensor_tensor(rstd[:, t:t + 1], msq[:, t:t + 1], neghalf[:, 0:1], ALU.pow).then_inc(rstd_ready, 1)

            def mask_na(l):
                pool.wait_ge(na_in, 256 * (l + 1))
                if l == 0:
                    pool.wait_ge(small_in, 16 * 16)
                for q in range(2):
                    for h in range(4):
                        v = bias_na[:, q, h, :].rearrange("p (a b) -> p a b", a=4)
                        pool.tensor_tensor(v, v, nmask[:, :].unsqueeze(1).broadcast_to([P, 4, 64]), ALU.add).then_inc(na_ready, 1)

            def mix(l):
                pool.wait_ge(mla_ms, l + 1)
                pool.tensor_tensor(rstd[:, 2:6], msq[:, 2:6], neghalf[:, 0:4], ALU.pow).then_inc(mla_rs, 1)
                pool.wait_ge(d_ms, l + 1)
                pool.tensor_tensor(drs[:, :], dms[:, :], neghalf[:, :], ALU.pow).then_inc(d_rs, 1)

            for v in range(5):
                rsqrt(v)
                if v == 3:
                    mask_na(0)
            rsqrt(5)
            mix(0)
            rsqrt(6)
            mask_na(1)
            rsqrt(7)
            mix(1)
            rsqrt(8)
            rsqrt(9)

        @block.scalar
        def _(act):
            def split(n, b=0):
                s = slot_of(n)
                act.wait_ge(raw_in[s], 16 * (n // SLOTS + 1 + b))
                if not (isinstance(b, int) and n + 3 * b < SLOTS):
                    act.wait_ge(units_used, n - 2 + 3 * b)
                if n in (MIX_U[0] + 1, MIX_U[1] + 1):
                    for dst, src in kr_parts(whi[:, s, :], raw[:, s, :]):
                        i = act.activation(dst, src, ACT.Copy)
                    i.then_inc(hi_ready, 1)
                else:
                    act.activation(whi[:, s, :], raw[:, s, :], ACT.Copy).then_inc(hi_ready, 1)

            def square(version, t, h):
                if version:
                    act.wait_ge(x_ready, 4 * (version - 1) + 2 * t + h + 1)
                    act.wait_ge(msq_ready, 2 * version)
                else:
                    act.wait_ge(x_in, 32)
                if version or t or h:
                    act.wait_ge(squares, 4 * version + 2 * t + h)
                act.activation(junk[:, :], x[:, t, h * HALF:(h + 1) * HALF], ACT.Square, scale=1.0 / 32,
                               accum_out=ssq[:, t, h:h + 1]).then_inc(squares, 1)

            def h_out(j, t, h):
                dst = o_hi if j == 2 else h_hi
                act.wait_ge(xT_ready, 4 * (HT_NO[j] - 1) + 2 * t + h + 1)
                act.activation(dst[:, 4 * h:4 * h + 4, t * P:(t + 1) * P],
                               bank[2 * t + h][:, :].rearrange("p (c k) -> p c k", c=4), ACT.Copy).then_inc(hT_hi, 1)

            def norm(j, square_too=True):
                for t in range(TT):
                    for h in range(2):
                        if square_too:
                            square(NORM_X[j], t, h)
                for t in range(TT):
                    for h in range(2):
                        h_out(j, t, h)

            def ffn(f):
                u0, e0 = FFN_U[f], NB * f
                norm([1, 4, 7, 9][f])

                def silu(b, par):
                    act.wait_ge(units_used, u0 + 3 * b)
                    act.wait_ge(glu_ready, e0 + b)
                    act.activation(sil, bank[2 * par][:, :], ACT.Silu).then_inc(silu_ready, 1)

                split(u0 + 2)
                split(u0 + 3)
                act.wait_ge(units_used, u0 + 1)
                if e0:
                    act.wait_ge(glu_ready, e0)
                else:
                    act.wait_ge(scratch_out, 64)
                act.activation(sil, bank[0][:, :], ACT.Silu).then_inc(silu_ready, 1)

                def block_steps(b, par):
                    for k in (1, 2, 3):
                        split(u0 + k, b)
                    silu(b, par)

                block_steps(1, 1)
                with act.Fori(2, NB - 1, 2) as b:
                    block_steps(b, 0)
                    block_steps(b + 1, 1)
                n = u0 + 3 * (NB - 1)
                for k in (1, 2, 3):
                    if n + k < N_UNITS:
                        split(n + k)
                silu(NB - 1, 0)
                if n + 4 < N_UNITS:
                    split(n + 4)

            def proj_copy(no, n, dst, bk, scale=1.0):
                act.wait_ge(units_used, n + 1)
                act.activation(dst, bk, ACT.Copy, scale=scale).then_inc(proj_out, 1)

            def exps(i, item, biased, width0=T):
                act.wait_ge(maxed, i + 1)
                s = i % 8
                for q in range(2):
                    w = width0 if q == 0 else T
                    src = pr[:, s, q, 0:w] if biased else bank[i % 2][:, q * T:q * T + w]
                    e = act.activation(pr[:, s, q, 0:w], src, ACT.Exp, bias=negmax[:, s, q:q + 1],
                                       scale=-1.0 if biased else 1.0, accum_out=psumrow[:, s, q:q + 1])
                e.then_inc(exped, 1)

            def pt_copy(q, head, width):
                act.wait_ge(transposed, q + 1)
                if head >= 4:
                    act.wait_ge(pv_done, head - 3)
                act.activation(pt[:, head % 4, 0:width], bank[2 + q % 2][:, 0:width], ACT.Copy).then_inc(pt_ready, 1)

            def o_copy(no, nheads, bk, chunk):
                act.wait_ge(pv_done, nheads)
                act.activation(o_hi[:, chunk:chunk + 2, :], bank[bk][:, :].rearrange("p (c k) -> p c k", c=2),
                               ACT.Copy).then_inc(out_hi, 1)

            for t in range(TT):
                for h in range(2):
                    square(0, t, h)
            split(0)
            for k in range(4):
                act.wait_ge(pool_d, k + 1)
                act.activation(h_hi[:, 2 * k:2 * k + 2, :], bank[k][:, :].rearrange("p (c k) -> p c k", c=2),
                               ACT.Copy).then_inc(hT_hi, 1)
            split(1)
            split(2)
            for l in range(2):
                act.wait_ge(lam_r, 2 * l + 2)
                act.activation(lam_e[:, l, :], lam_s[:, l, :], ACT.Exp).then_inc(lam_x, 1)
            ffn(0)

            for ev in moba_script():
                k = ev[0]
                if k == "q_norm":
                    norm(2)
                elif k == "kv_norm":
                    norm(3, False)
                elif k == "split":
                    split(MOBA_U + ev[1])
                elif k == "proj" and ev[1] < 12:
                    n = ev[1]
                    par = ((n - 4) // 2) % 2
                    bk = bank[4 + n % 2]
                    if n < 4:
                        proj_copy(n, MOBA_U + n, qall[:, 2 * n:2 * n + 2, :].rearrange("p a b -> p (a b)"), bk[:, :], HD ** -0.5)
                    elif n % 2 == 0:
                        if n >= 8:
                            act.wait_ge(scores, 4 * ((n - 4) // 2) - 4)
                        proj_copy(n, MOBA_U + n, kg[:, par].rearrange("p a b -> p (a b)"), bk[:, :])
                    else:
                        if n >= 9:
                            act.wait_ge(pv_done, 4 * ((n - 4) // 2) - 4)
                        proj_copy(n, MOBA_U + n, vg[:, par].rearrange("p a b -> p (a b)"), bk[:, :])
                elif k == "S":
                    exps(ev[1], ev[1], True, P)
                elif k == "T":
                    pt_copy(ev[1], ev[1], 3 * P)
                elif k == "O":
                    g = ev[1]
                    o_copy(g, 4 * g + 4, 0 if g == 3 else 6 + g % 2, 2 * g)
            ffn(1)

            def mix(l):
                i0, q0, p0 = stage_items(l)
                hd0 = 16 + 16 * l
                u0 = MIX_U[l]
                if l == 0:
                    for t in range(TT):
                        for h in range(2):
                            square(4, t, h)
                norm(6 + 2 * l)
                nt = 0
                for ev in mix_script():
                    k = ev[0]
                    if k == "split":
                        split(u0 + ev[1])
                    elif k == "proj":
                        n = ev[1]
                        bk = bank[(6 if n < 2 else 4) + n % 2]
                        if n == 0:
                            act.wait_ge(units_used, u0 + 1)
                            act.wait_ge(squares, 4 * NORM_X[6 + 2 * l] + 4)
                            for t in range(TT):
                                if l or t:
                                    act.wait_ge(mla_sq, 4 * l + t)
                                act.activation(junk[:, 0:MLA_QR], bk[:, t * T:t * T + MLA_QR], ACT.Square, scale=MLA_QR ** -0.5,
                                               accum_out=msm[:, t:t + 1]).then_inc(mla_sq, 1)
                        elif n == 1:
                            act.wait_ge(units_used, u0 + 2)
                            for t in range(TT):
                                act.wait_ge(mla_sq, 4 * l + 2 + t)
                                act.activation(junk[:, 0:MLA_KVR], bk[:, t * P:t * P + P], ACT.Square, scale=MLA_KVR ** -0.5,
                                               accum_out=msm[:, 2 + t:3 + t]).then_inc(mla_sq, 1)
                        elif n < 11:
                            g, kind = (n - 2) // 3, (n - 2) % 3
                            par = (g + 1) % 2
                            dst = (kg, qg, vg)[kind][:, par].rearrange("p a b -> p (a b)")
                            scale = 1.0
                            if kind == 1:
                                scale = (ROPE if g == 1 else HD) ** -0.5
                            if kind < 2 and g == 2:
                                act.wait_ge(scores, i0 + 8)
                            if kind == 2 and g:
                                act.wait_ge(pv_done, hd0 + 4 * g)
                            proj_copy(n, u0 + n, dst, bk[:, :], scale)
                    elif k == "mla_T":
                        act.wait_ge(small_in, 16 * 16)
                        act.wait_ge(mla_t, l + 1)
                        for cc in range(3):
                            src = bank[0][:, cc * T:(cc + 1) * T] if cc < 2 else bank[1][:, 0:T]
                            e = act.activation(latT[:, cc, :], src, ACT.Copy, scale=mlag[:, l, cc:cc + 1])
                        e.then_inc(mla_tT, 1)
                    elif k == "mla_G":
                        act.wait_ge(mla_g, 3 * l + 1)
                        for c2 in range(2):
                            act.activation(qall[0:HD, 2 * c2:2 * c2 + 2, :], bank[c2][0:HD, :].rearrange("p (c k) -> p c k", c=2),
                                           ACT.Copy, scale=MLA_D ** -0.5)
                        act.wait_ge(mla_g, 3 * l + 2)
                        for c2 in range(2):
                            act.activation(qall[0:HD, 4 + 2 * c2:6 + 2 * c2, :], bank[2 + c2][0:HD, :].rearrange("p (c k) -> p c k", c=2), ACT.Copy)
                        act.wait_ge(mla_g, 3 * l + 3)
                        act.activation(vg[:, 0].rearrange("p a b -> p (a b)"), bank[6][:, :], ACT.Copy).then_inc(mla_copied, 1)
                    elif k == "S":
                        exps(i0 + ev[1], ev[1], ev[1] >= 4)
                    elif k == "T":
                        pt_copy(q0 + nt, hd0 + ev[1], 2 * T)
                        nt += 1
                    elif k == "diff_stats":
                        act.wait_ge(pv_done, hd0 + 12)
                        act.activation(dsquare, bank[6][:, :], ACT.Square, scale=HD ** -0.5).then_inc(d_sq, 1)
                    elif k == "diff_T":
                        act.wait_ge(transposed, q0 + nt + 1)
                        act.wait_ge(lam_done, 2)
                        act.activation(o_hi[:, 2:4, :], bank[2 + (q0 + nt) % 2][:, :].rearrange("p (c k) -> p c k", c=2),
                                       ACT.Copy, scale=subln_s[:, l:l + 1]).then_inc(pt_ready, 1)
                        nt += 1
                    elif k == "O":
                        g = ev[1]
                        o_copy(OUT_HI[l][g], hd0 + 4 * g + 4, [6, 7, None, 0][g], MIX_OUT_CHUNK[g])

            mix(0)
            ffn(2)
            mix(1)
            ffn(3)
            for t in range(TT):
                for h in range(2):
                    square(9, t, h)

        @block.vector
        def _(dve):
            chained = [0]

            def then_wait(i):
                chained[0] += 1
                i.then_inc(vchain, 1)
                dve.wait_ge(vchain, chained[0])

            def split(n, b=0):
                s = slot_of(n)
                dve.wait_ge(hi_ready, n + 1 + 3 * b)
                if n in (MIX_U[0] + 1, MIX_U[1] + 1):
                    parts = zip(kr_parts(wlo[:, s, :], raw[:, s, :]), kr_parts(whi[:, s, :], raw[:, s, :]))
                    for (dst, src), (hi, _) in parts:
                        i = dve.tensor_tensor(dst, src, hi.bitcast(F32), ALU.subtract)
                    i.then_inc(lo_ready, 1)
                else:
                    dve.tensor_tensor(wlo[:, s, :], raw[:, s, :], whi[:, s, :].bitcast(F32), ALU.subtract).then_inc(lo_ready, 1)

            def add_residual(version, t, h):
                if (t, h) == (1, 1):
                    dve.wait_ge(units_used, LAST_U[version] + 1)
                else:
                    dve.wait_ge(acc_ready, 3 * ACC_NO[version] + 2 * t + h + 1)
                if version == 1 and (t, h) == (0, 0):
                    dve.wait_ge(small_in, 16 * 16)
                xs = x[:, t, h * HALF:(h + 1) * HALF]
                acc = bank[ACC[2 * t + h]][:, :]
                if version == 1:
                    tmp = pr[:, 7, :, :].rearrange("p a b -> p (a b)")
                    if t or h:
                        dve.wait_ge(x_ready, 2 * t + h)
                    then_wait(dve.tensor_tensor(tmp, acc, pt[:, h, :], ALU.mult))
                    dve.tensor_tensor(xs, xs, tmp, ALU.add).then_inc(x_ready, 1)
                else:
                    dve.tensor_tensor(xs, xs, acc, ALU.add).then_inc(x_ready, 1)

            def mean_square(version, t):
                dve.wait_ge(squares, 4 * version + 2 * t + 2)
                if version:
                    dve.wait_ge(rstd_ready, 2 * version)
                dve.tensor_scalar(msq[:, t:t + 1], ssq[:, t, 0:1], ssq[:, t, 1:2], EPS, ALU.add, ALU.add).then_inc(msq_ready, 1)

            def normalise(j, t, h):
                if (t, h) == (0, 0):
                    dve.wait_ge(gains_in[j % 2], 16 * (j // 2 + 1))
                dve.wait_ge(rstd_ready, 2 * NORM_X[j] + t + 1)
                if j in XN_NO and XN_NO[j] > 1:
                    dve.wait_ge(xT_ready, 4 * (HT_NO[j] - 2) + 2 * t + 2)
                cols = slice(h * HALF, (h + 1) * HALF)
                dst = x if j == 5 else xn
                done = x_ready if j == 5 else fin if j == 10 else xn_ready
                dve.scalar_tensor_tensor(out=dst[:, t, cols], in0=x[:, t, cols], scalar=rstd[:, t:t + 1],
                                         in1=gains[:, j % 2, cols], op0=ALU.mult, op1=ALU.mult).then_inc(done, 1)

            def h_lo_out(j, t, h):
                dst, hi = (o_lo, o_hi) if j == 2 else (h_lo, h_hi)
                dve.wait_ge(hT_hi, 4 * HT_NO[j] + 2 * t + h + 1)
                cols = (slice(None), slice(4 * h, 4 * h + 4), slice(t * P, (t + 1) * P))
                dve.tensor_tensor(dst[cols], bank[2 * t + h][:, :].rearrange("p (c k) -> p c k", c=4),
                                  hi[cols].bitcast(F32), ALU.subtract).then_inc(hT_lo, 1)

            def norm(j, residual=True, stats=True):
                v = NORM_X[j]
                if residual:
                    add_residual(v, 0, 0)
                    add_residual(v, 0, 1)
                if stats:
                    mean_square(v, 0)
                if residual:
                    add_residual(v, 1, 0)
                normalise(j, 0, 0)
                if residual:
                    add_residual(v, 1, 1)
                normalise(j, 0, 1)
                if stats:
                    mean_square(v, 1)
                h_lo_out(j, 0, 0)
                normalise(j, 1, 0)
                normalise(j, 1, 1)
                h_lo_out(j, 0, 1)
                h_lo_out(j, 1, 0)
                h_lo_out(j, 1, 1)

            def ffn(f):
                u0, e0 = FFN_U[f], NB * f
                norm([1, 4, 7, 9][f])
                if f:
                    split(u0 + 1)

                def glu(b, par):
                    dve.wait_ge(silu_ready, e0 + b + 1)
                    if not (isinstance(b, int) and e0 + b == 0):
                        dve.wait_ge(act_ready, e0 + b)
                    dve.wait_ge(units_used, (u0 + 2 if isinstance(b, int) and b == 0 else u0 + 1 + 3 * b))
                    dve.tensor_tensor(act32, sil, bank[2 * par + 1][:, :], ALU.mult).then_inc(glu_ready, 1)
                    dve.wait_ge(glu_ready, e0 + b + 1)
                    hi = o_hi[:, 2 * par:2 * par + 2, :].rearrange("p a b -> p (a b)")
                    lo = o_lo[:, 2 * par:2 * par + 2, :].rearrange("p a b -> p (a b)")
                    if not isinstance(b, int) or b >= 2:
                        dve.wait_ge(units_used, u0 - 1 + 3 * b)
                    dve.tensor_copy(hi, act32).then_inc(act_hi, 1)
                    dve.wait_ge(act_hi, e0 + b + 1)
                    dve.tensor_tensor(lo, act32, hi.bitcast(F32), ALU.subtract).then_inc(act_ready, 1)

                split(u0 + 2)
                split(u0 + 3)
                glu(0, 0)

                def block_steps(b, par):
                    for k in (1, 2, 3):
                        split(u0 + k, b)
                    glu(b, par)

                block_steps(1, 1)
                with dve.Fori(2, NB - 1, 2) as b:
                    block_steps(b, 0)
                    block_steps(b + 1, 1)
                n = u0 + 3 * (NB - 1)
                for k in (1, 2, 3):
                    if n + k < N_UNITS:
                        split(n + k)
                glu(NB - 1, 0)

            def maxima(i, biases, width0=T):
                s = i % 8
                dve.wait_ge(scores, i + 1)
                if i >= 8:
                    dve.wait_ge(transposed, T_BEFORE[i])
                if biases is None:
                    dve.tensor_reduce(negmax[:, s, :], bank[i % 2][:, :].rearrange("p (q k) -> p q k", q=2), AX_X,
                                      ALU.max, negate=True).then_inc(maxed, 1)
                    return
                for q in range(2):
                    w = width0 if q == 0 else T
                    e = dve.tensor_tensor_reduce(pr[:, s, q, 0:w], bank[i % 2][:, q * T:q * T + w], biases[q], -1.0, BIG,
                                                 ALU.add, ALU.min, negmax[:, s, q:q + 1])
                e.then_inc(maxed, 1)

            def normal(i, width0=T, lam=None):
                s = i % 8
                dve.wait_ge(exped, i + 1)
                then_wait(dve.reciprocal(rsum[:, s, :], psumrow[:, s, :]))
                if lam is None:
                    for q in range(2):
                        w = width0 if q == 0 else T
                        e = dve.tensor_scalar(pr[:, s, q, 0:w], pr[:, s, q, 0:w], rsum[:, s, q:q + 1], None, ALU.mult)
                    e.then_inc(normed, 1)
                else:
                    then_wait(dve.tensor_scalar(rsum[:, s, :], rsum[:, s, :], lam, None, ALU.mult))
                    dve.wait_ge(normed, i)
                    for q in range(2):
                        e = dve.scalar_tensor_tensor(out=pr[:, s - 1, q, :], in0=pr[:, s, q, :], scalar=rsum[:, s, q:q + 1],
                                                     in1=pr[:, s - 1, q, :], op0=ALU.mult, op1=ALU.add)
                    e.then_inc(normed, 1)

            def o_low(no, bk, chunk):
                dve.wait_ge(out_hi, no + 1)
                dve.tensor_tensor(o_lo[:, chunk:chunk + 2, :], bank[bk][:, :].rearrange("p (c k) -> p c k", c=2),
                                  o_hi[:, chunk:chunk + 2, :].bitcast(F32), ALU.subtract).then_inc(out_lo, 1)

            dve.memset(tab_moba[NBUCKET:NBUCKET + 1, :], 1.0).then_inc(ones_set, 1)
            dve.memset(tab_t5[NBUCKET:NBUCKET + 1, :], 1.0).then_inc(ones_set, 1)
            for t in range(TT):
                mean_square(0, t)
            for t in range(TT):
                for h in range(2):
                    normalise(0, t, h)
            split(0)
            for i, nr in enumerate((16, 4, 4)):
                dve.wait_ge(vec_done, i + 1)
                dve.tensor_copy(vecs[0:nr, i, 0:SEQ_D], bank[4 + i][0:nr, :]).then_inc(vec_out, 1)
            for k in range(4):
                dve.wait_ge(hT_hi, k + 1)
                dve.tensor_tensor(h_lo[:, 2 * k:2 * k + 2, :], bank[k][:, :].rearrange("p (c k) -> p c k", c=2),
                                  h_hi[:, 2 * k:2 * k + 2, :].bitcast(F32), ALU.subtract).then_inc(hT_lo, 1)
            split(1)
            split(2)
            dve.wait_ge(small_in, 16 * 16)
            for l in range(2):
                for r in range(2):
                    dve.tensor_tensor_reduce(lam_in[:, l, 64 * r:64 * r + 32], lam_in[:, l, 64 * r:64 * r + 32],
                                             lam_in[:, l, 64 * r + 32:64 * r + 64], 1.0, 0.0, ALU.mult, ALU.add,
                                             lam_s[:, l, r:r + 1]).then_inc(lam_r, 1)
            for l in range(2):
                init = 0.8 - 0.6 * math.exp(-0.3 * l)
                dve.wait_ge(lam_x, l + 1)
                dve.tensor_scalar(neglam[:, l:l + 1], lam_e[:, l, 1:2], lam_e[:, l, 0:1], -init, ALU.subtract, ALU.add)
                dve.tensor_scalar(subln_s[:, l:l + 1], subln[:, l:l + 1], 1.0 - init, None, ALU.mult).then_inc(lam_done, 1)
            dve.wait_ge(lam_done, 2)
            ffn(0)

            for ev in moba_script():
                k = ev[0]
                if k == "q_norm":
                    norm(2)
                    split(MOBA_U + 1)
                elif k == "kv_norm":
                    norm(3, residual=False, stats=False)
                elif k == "split" and ev[1] < 17:
                    split(MOBA_U + ev[1])
                elif k == "S":
                    i = ev[1]
                    if i == 0:
                        dve.wait_ge(bias_in, 16)
                    maxima(i, [down_from(bias_moba[:, i, :], P - 1, P), down_from(bias_moba[:, i, :], T - 1, T)], P)
                elif k == "N":
                    normal(ev[1], P)
                elif k == "O":
                    g = ev[1]
                    o_low(g, 0 if g == 3 else 6 + g % 2, 2 * g)
            ffn(1)

            def final_norm_1():
                for h in range(2):
                    add_residual(4, 0, h)
                mean_square(4, 0)
                add_residual(4, 1, 0)
                add_residual(4, 1, 1)
                normalise(5, 0, 0)
                normalise(5, 0, 1)
                mean_square(4, 1)
                mean_square(5, 0)
                normalise(5, 1, 0)
                normalise(5, 1, 1)
                normalise(6, 0, 0)
                normalise(6, 0, 1)
                mean_square(5, 1)
                h_lo_out(6, 0, 0)
                h_lo_out(6, 0, 1)
                for h in range(2):
                    normalise(6, 1, h)
                for h in range(2):
                    h_lo_out(6, 1, h)

            def mix(l):
                i0, q0, p0 = stage_items(l)
                u0 = MIX_U[l]
                if l == 0:
                    final_norm_1()
                else:
                    norm(8)
                split(u0 + 1)
                for ev in mix_script():
                    k = ev[0]
                    if k == "split" and ev[1] < 16:
                        split(u0 + ev[1])
                    elif k == "proj" and ev[1] == 1:
                        dve.wait_ge(mla_sq, 4 * l + 4)
                        dve.tensor_scalar(msq[:, 2:6], msm[:, 0:4], EPS, None, ALU.add).then_inc(mla_ms, 1)
                        dve.wait_ge(mla_rs, l + 1)
                        for t in range(TT):
                            dve.tensor_scalar(latq(t), bank[6][:, t * T:(t + 1) * T], rstd[:, 2 + t:3 + t], None, ALU.mult)
                            e = dve.tensor_scalar(latkv(t), bank[7][:, t * P:(t + 1) * P], rstd[:, 4 + t:5 + t], None, ALU.mult)
                        e.then_inc(mla_lat, 1)
                        for r in range(2):
                            rr = slice(64 + 32 * r, 96 + 32 * r)
                            e = dve.tensor_tensor(ropet[64:96, r, 0:T], bank[7][rr, T:2 * T], rope[rr, 1, :], ALU.mult)
                        e.then_inc(mla_rope, 1)
                        dve.wait_ge(mla_rope, 4 * l + 1)
                        if l:
                            dve.wait_ge(scores, i0 - 16)
                        dve.tensor_tensor(qall[64:96, 4:8, :], ropet[64:96, 0, 0:T].unsqueeze(1).broadcast_to([32, 4, T]),
                                          ropet[64:96, 1, 0:T].unsqueeze(1).broadcast_to([32, 4, T]), ALU.add).then_inc(mla_rope, 1)
                    elif k == "mla_G":
                        dve.wait_ge(mla_g, 3 * l + 1)
                        dve.wait_ge(mla_rope, 4 * l + 2)
                        for c2 in range(2):
                            for r in range(2):
                                rr = slice(64 + 32 * r, 96 + 32 * r)
                                e = dve.tensor_tensor(ropet[64:96, r, :].rearrange("p (c k) -> p c k", c=2),
                                                      bank[c2][rr, :].rearrange("p (c k) -> p c k", c=2),
                                                      rope[rr, 0, :].unsqueeze(1).broadcast_to([32, 2, T]), ALU.mult)
                            then_wait(e)
                            e = dve.tensor_tensor(qall[64:96, 2 * c2:2 * c2 + 2, :],
                                                  ropet[64:96, 0, :].rearrange("p (c k) -> p c k", c=2),
                                                  ropet[64:96, 1, :].rearrange("p (c k) -> p c k", c=2), ALU.add)
                            e.then_inc(mla_rope, 1)
                            dve.wait_ge(mla_rope, 4 * l + 3 + c2)
                    elif k == "S":
                        i = ev[1]
                        if i < 4:
                            b = None
                        elif i < 8:
                            if i == 4:
                                dve.wait_ge(na_ready, 8 * (l + 1))
                            b = [down_from(bias_na[:, q, i - 4, :], T - 1, T) for q in range(2)]
                        else:
                            if i == 8:
                                dve.wait_ge(bias2_in, 32)
                            t5 = bias_diff[:, (i - 8) // 2, :] if i < 16 else bias_dil[:, i - 16, :]
                            b = [down_from(t5, T - 1, T), down_from(t5, T + P - 1, T)]
                        maxima(i0 + i, b)
                    elif k == "N":
                        i = ev[1]
                        second = 8 <= i < 16 and i % 2
                        normal(i0 + i, T, neglam[:, l:l + 1] if second else None)
                    elif k == "diff_stats":
                        dve.wait_ge(d_sq, l + 1)
                        dve.tensor_reduce(dsq[:, :], dsquare.rearrange("p (g n) -> p g n", n=HD), AX_X, ALU.add).then_inc(d_red, 1)
                        dve.wait_ge(d_red, l + 1)
                        dve.tensor_scalar(dms[:, :], dsq[:, :], EPS, None, ALU.add).then_inc(d_ms, 1)
                    elif k == "diff_norm":
                        dve.wait_ge(d_rs, l + 1)
                        dve.tensor_tensor(dno.rearrange("p (g n) -> p g n", n=HD), bank[6][:, :].rearrange("p (g n) -> p g n", n=HD),
                                          drs[:, :].unsqueeze(2).broadcast_to([P, 8, HD]), ALU.mult).then_inc(d_n, 1)
                    elif k == "diff_T":
                        q = q0 + T_DIFF
                        dve.wait_ge(pt_ready, q + 1)
                        dve.scalar_tensor_tensor(out=o_lo[:, 2:4, :].rearrange("p a b -> p (a b)"), in0=bank[2 + q % 2][:, :],
                                                 scalar=subln_s[:, l:l + 1],
                                                 in1=o_hi[:, 2:4, :].bitcast(F32).rearrange("p a b -> p (a b)"),
                                                 op0=ALU.mult, op1=ALU.subtract).then_inc(out_lo, 1)
                    elif k == "O":
                        g = ev[1]
                        o_low(OUT_HI[l][g], [6, 7, None, 0][g], MIX_OUT_CHUNK[g])

            mix(0)
            ffn(2)
            mix(1)
            ffn(3)
            add_residual(9, 0, 0)
            add_residual(9, 0, 1)
            mean_square(9, 0)
            add_residual(9, 1, 0)
            normalise(10, 0, 0)
            add_residual(9, 1, 1)
            mean_square(9, 1)
            normalise(10, 0, 1)
            for h in range(2):
                normalise(10, 1, h)

        @block.tensor
        def _(pe):
            def three(dst, ahi, alo, bhi, blo, first, last):
                pe.matmul(dst, ahi, bhi, start=first, stop=False)
                pe.matmul(dst, ahi, blo, start=False, stop=False)
                return pe.matmul(dst, alo, bhi, start=False, stop=last)

            def w8(n, width=FB):
                s = slot_of(n)
                return tuple(w[:, s, 0:KC * width].rearrange("p (k n) -> p k n", k=KC) for w in (whi, wlo))

            def w2(n):
                s = slot_of(n)
                return tuple(w[:, s, :].rearrange("p (k n) -> p k n", k=2) for w in (whi, wlo))

            def feature_major(n, bk, toks, j, src):
                hi, lo = w8(n)
                for kc in range(KC):
                    mm = three(bank[bk][:, j * T + toks.start:j * T + toks.stop],
                               hi[:, kc, j * P:(j + 1) * P], lo[:, kc, j * P:(j + 1) * P],
                               src[0][:, kc, toks], src[1][:, kc, toks], kc == 0, kc == KC - 1)
                return mm

            def token_major(n, bk, col, width, t, src, wcols, total=FB):
                hi, lo = w8(n, total)
                for kc in range(KC):
                    mm = three(bank[bk][:, col:col + width], src[0][:, kc, t * P:(t + 1) * P], src[1][:, kc, t * P:(t + 1) * P],
                               hi[:, kc, wcols], lo[:, kc, wcols], kc == 0, kc == KC - 1)
                return mm

            def residual(n, chunks, src, first, last):
                hi, lo = w2(n)
                for t in range(TT):
                    for h in range(2):
                        for k in range(2):
                            mm = three(bank[ACC[2 * t + h]][:, :], src[0][:, chunks + k, t * P:(t + 1) * P],
                                       src[1][:, chunks + k, t * P:(t + 1) * P], hi[:, k, h * HALF:(h + 1) * HALF],
                                       lo[:, k, h * HALF:(h + 1) * HALF], first and k == 0, last and k == 1)
                        if last and (t, h) != (1, 1):
                            mm.then_inc(acc_ready, 1)
                return mm

            def used(bump):
                bump.then_inc(units_used, 1)

            def transposes(j, t):
                for h in range(2):
                    pe.wait_ge(xn_ready, 4 * XN_NO[j] + 2 * t + h + 1)
                    if HT_NO[j] == 3:
                        pe.wait_ge(hT_lo, 4 * 2 + 2 * t + h + 1)
                    for k in range(4):
                        mm = pe.transpose(bank[2 * t + h][:, k * P:(k + 1) * P],
                                          xn[:, t, (4 * h + k) * P:(4 * h + k + 1) * P], ident[:, :])
                    mm.then_inc(xT_ready, 1)

            H = (h_hi, h_lo)
            O = (o_hi, o_lo)
            ALL = slice(0, T)

            def tile(t):
                return slice(t * P, (t + 1) * P)

            def wait_h(j, t):
                pe.wait_ge(hT_lo, 4 * HT_NO[j] + 2 * t + 2)

            pe.wait_ge(ones_set, 2)
            pe.wait_ge(table_in, 32)
            pe.wait_ge(onehot_in, 48)
            K = NBUCKET + 1
            for i, lhs in enumerate((tab_moba[0:K, :], tab_t5[0:K, 0:4], tab_t5[0:K, 4:8])):
                pe.matmul(bank[4 + i][0:lhs.shape[1], :], lhs, onehots[0:K, i, :], start=True, stop=True).then_inc(vec_done, 1)

            pe.wait_ge(band_in, 16)
            pe.wait_ge(xn_ready, 4)
            for g in range(4):
                for k in range(2):
                    for s in range(TT):
                        mm = pe.matmul(bank[g][:, k * T:(k + 1) * T], xn[:, s, g * 256 + k * P:g * 256 + (k + 1) * P],
                                       band[:, g, s, :], start=(s == 0), stop=(s == TT - 1))
                mm.then_inc(pool_d, 1)
            pe.wait_ge(lo_ready, 1)
            pe.wait_ge(vec_out, 3)
            hi, lo = w8(POOL_U)
            for t in range(TT):
                for h in range(2):
                    for g in (2 * h, 2 * h + 1):
                        pe.wait_ge(hT_lo, g + 1)
                        for k in range(2):
                            mm = three(bank[ACC[2 * t + h]][:, (g % 2) * 256:(g % 2) * 256 + 256],
                                       h_hi[:, 2 * g + k, tile(t)], h_lo[:, 2 * g + k, tile(t)],
                                       hi[:, 2 * g + k, :], lo[:, 2 * g + k, :], k == 0, k == 1)
                    if (t, h) != (1, 1):
                        mm.then_inc(acc_ready, 1)
            used(mm)

            def ffn(f):
                u0, e0 = FFN_U[f], NB * f
                j = [1, 4, 7, 9][f]
                if f == 0:
                    pe.wait_ge(small_in, 16 * 16)
                for t in range(TT):
                    transposes(j, t)
                wait_h(j, 1)
                for u in range(2):
                    pe.wait_ge(lo_ready, u0 + u + 1)
                    for jj in range(2):
                        mm = feature_major(u0 + u, u, ALL, jj, H)
                    used(mm)

                def gate_up(b, par, off):
                    for u in range(2):
                        pe.wait_ge(lo_ready, u0 + 3 * b + u)
                        if off >= 2:
                            pe.wait_ge(glu_ready, e0 + b - 1)
                        for jj in range(2):
                            mm = feature_major(u0 - 1 + u, 2 * par + u, ALL, jj, H)
                        used(mm)

                def down(b, par, k, first=False, last=False):
                    pe.wait_ge(act_ready, e0 + b + 1)
                    pe.wait_ge(lo_ready, k + 1)
                    used_slot = (u0 + 1) if not last else (u0 + 3 * NB - 1)
                    return residual(used_slot, 2 * par, O, first, last)

                gate_up(1, 1, 1)
                used(down(0, 0, u0 + 4, first=True))
                with pe.Fori(2, NB - 1, 2) as b:
                    gate_up(b, 0, 2)
                    used(down(b - 1, 1, u0 + 1 + 3 * b))
                    gate_up(b + 1, 1, 2)
                    used(down(b, 0, u0 + 4 + 3 * b))
                b = NB - 1
                gate_up(b, 0, 2)
                used(down(b - 1, 1, u0 + 1 + 3 * b))
                used(down(b, 0, u0 + 2 + 3 * b, last=True))

            ffn(0)

            def scores_of(i, q, k, causal):
                if i >= 2:
                    pe.wait_ge(exped, i - 1)
                for qt in range(2):
                    w = P if causal and qt == 0 else T
                    mm = pe.matmul(bank[i % 2][:, qt * T:qt * T + w], q[:, qt * P:(qt + 1) * P], k[:, 0:w], start=True, stop=True)
                mm.then_inc(scores, 1)

            def transpose_head(q, i, causal):
                if q >= 2:
                    pe.wait_ge(pt_ready, q - 1)
                at = 0
                for kt in range(2):
                    for qt in range(2):
                        if causal and kt > qt:
                            continue
                        mm = pe.transpose(bank[2 + q % 2][:, at:at + P], pr[:, i % 8, qt, kt * P:(kt + 1) * P], ident[:, :])
                        at += P
                mm.then_inc(transposed, 1)

            def head_out(head, q, h, bk, v, causal):
                pe.wait_ge(pt_ready, q + 1)
                rows = slice((h % 2) * HD, (h % 2) * HD + HD)
                c0 = (h // 2) * T
                p = pt[:, head % 4, :]
                pe.matmul(bank[bk][rows, c0:c0 + T], v[:, 0, h * HD:(h + 1) * HD], p[:, 0:T], start=True, stop=False)
                if causal:
                    mm = pe.matmul(bank[bk][rows, c0 + P:c0 + T], v[:, 1, h * HD:(h + 1) * HD], p[:, T:T + P], start=False, stop=True)
                else:
                    mm = pe.matmul(bank[bk][rows, c0:c0 + T], v[:, 1, h * HD:(h + 1) * HD], p[:, T:2 * T], start=False, stop=True)
                mm.then_inc(pv_done, 1)

            for ev in moba_script():
                k = ev[0]
                if k == "q_norm":
                    for t in range(TT):
                        transposes(2, t)
                elif k == "kv_norm":
                    for t in range(TT):
                        transposes(3, t)
                elif k == "unit":
                    n = ev[1]
                    u = MOBA_U + n
                    pe.wait_ge(lo_ready, u + 1)
                    if n < 12:
                        if n >= 2:
                            pe.wait_ge(proj_out, n - 1)
                        if n == 0:
                            wait_h(2, 1)
                        if n == 4:
                            wait_h(3, 1)
                        for x2 in range(2):
                            if n < 4:
                                mm = feature_major(u, 4 + n % 2, ALL, x2, O)
                            elif n % 2 == 0:
                                mm = feature_major(u, 4 + n % 2, ALL, x2, H)
                            else:
                                mm = token_major(u, 4 + n % 2, x2 * FB, FB, x2, H, slice(0, FB))
                        used(mm)
                    else:
                        if n == 12:
                            pe.wait_ge(proj_out, 12)
                        pe.wait_ge(out_lo, 3 if n == 12 else n - 11)
                        mm = residual(u, 2 * (n - 12), O, n == 12, n == 15)
                        used(mm)
                elif k == "S":
                    i = ev[1]
                    g, h = i // 4, i % 4
                    rows = slice((h % 2) * HD, (h % 2) * HD + HD)
                    pe.wait_ge(proj_out, 5 + 2 * g)
                    scores_of(i, qall[rows, 2 * g + h // 2, :], kg[rows, g % 2, h // 2, :], True)
                elif k == "T":
                    pe.wait_ge(normed, ev[1] + 1)
                    transpose_head(ev[1], ev[1], True)
                elif k == "V":
                    i = ev[1]
                    g = i // 4
                    if i % 4 == 0:
                        pe.wait_ge(proj_out, 6 + 2 * g)
                        if g == 2:
                            pe.wait_ge(out_lo, 1)
                        if g == 3:
                            pe.wait_ge(exped, 16)
                    head_out(i, i, i % 4, 0 if g == 3 else 6 + g % 2, vg[:, g % 2], True)
            ffn(1)

            def mix(l):
                i0, q0, p0 = stage_items(l)
                hd0 = 16 + 16 * l
                u0 = MIX_U[l]
                j = 6 + 2 * l
                for t in range(TT):
                    transposes(j, t)
                nt = 0
                t_of = {}
                for ev in mix_script():
                    k = ev[0]
                    if k == "unit":
                        n = ev[1]
                        u = u0 + n
                        bk = (6 if n < 2 else 4) + n % 2
                        pe.wait_ge(lo_ready, u + 1)
                        if n == 0:
                            wait_h(j, 1)
                        if 4 <= n < 11:
                            pe.wait_ge(proj_out, p0 + n - 3)
                        if n == 1:
                            for t in range(TT):
                                token_major(u, bk, t * P, P, t, H, slice(0, P), 192)
                            hi, lo = w8(u, 192)
                            for kc in range(KC):
                                mm = three(bank[bk][:, T:2 * T], hi[:, kc, 64:192], lo[:, kc, 64:192],
                                           h_hi[:, kc, :], h_lo[:, kc, :], kc == 0, kc == KC - 1)
                            used(mm)
                        elif n == 0 or (n < 11 and (n - 2) % 3 == 2):
                            for t in range(TT):
                                mm = token_major(u, bk, t * FB, FB, t, H, slice(0, FB))
                            used(mm)
                        elif n < 11:
                            for x2 in range(2):
                                mm = feature_major(u, bk, ALL, x2, H)
                            used(mm)
                        else:
                            if n == 11:
                                pe.wait_ge(proj_out, p0 + 9)
                                pe.wait_ge(d_n, l + 1)
                                pe.wait_ge(out_lo, OUT_LO[l][1] + 1)
                            else:
                                pe.wait_ge(out_lo, OUT_LO[l][n - 11] + 1)
                            mm = residual(u, MIX_OUT_CHUNK[n - 11], O, n == 11, n == 14)
                            used(mm)
                    elif k == "mla_T":
                        pe.wait_ge(mla_lat, l + 1)
                        for cc in range(3):
                            for t in range(TT):
                                dst = bank[0][:, cc * T + t * P:cc * T + (t + 1) * P] if cc < 2 else bank[1][:, t * P:(t + 1) * P]
                                src = latq(t)[:, cc * P:(cc + 1) * P] if cc < 2 else latkv(t)
                                mm = pe.transpose(dst, src, ident[:, :])
                        mm.then_inc(mla_t, 1)
                    elif k == "mla_G":
                        pe.wait_ge(mla_tT, l + 1)
                        pe.wait_ge(layer_in[l], 16 * 7)
                        for h in range(4):
                            for kc in range(2):
                                mm = pe.matmul(bank[h // 2][:, (h % 2) * T:(h % 2 + 1) * T], wuq[:, kc, h, :], latT[:, kc, :],
                                               start=(kc == 0), stop=(kc == 1))
                        mm.then_inc(mla_g, 1)
                        for h in range(4):
                            mm = pe.matmul(bank[2 + h // 2][0:HD, (h % 2) * T:(h % 2 + 1) * T], wukv[:, h, 0, :], latT[:, 2, :],
                                           start=True, stop=True)
                        mm.then_inc(mla_g, 1)
                        for t in range(TT):
                            mm = pe.matmul(bank[6][:, t * T:(t + 1) * T], latT[:, 2, tile(t)], wukv[:, :, 1, :], start=True, stop=True)
                        mm.then_inc(mla_g, 1)
                    elif k == "S":
                        i = ev[1]
                        if i == 0:
                            pe.wait_ge(mla_copied, l + 1)
                            pe.wait_ge(mla_rope, 4 * l + 4)
                        if i < 4:
                            q, kk = qall[0:MLA_D, i, :], qall[0:MLA_D, 4 + i, :]
                        else:
                            g = 0 if i < 8 else 1 if i < 16 else 2
                            pe.wait_ge(proj_out, p0 + 3 * g + 2)
                            par = (g + 1) % 2
                            if g == 1:
                                h, comp = (i - 8) // 2, i % 2
                                rows = slice((h % 2) * HD + comp * 32, (h % 2) * HD + comp * 32 + 32)
                            else:
                                h = i % 4
                                rows = slice((h % 2) * HD, (h % 2) * HD + HD)
                            q, kk = qg[rows, par, h // 2, :], kg[rows, par, h // 2, :]
                        scores_of(i0 + i, q, kk, False)
                    elif k == "T":
                        h = ev[1]
                        item = h if h < 8 else 8 + 2 * (h - 8) if h < 12 else h + 4
                        pe.wait_ge(normed, i0 + item + (2 if 8 <= h < 12 else 1))
                        if nt == T_DIFF + 2:
                            pe.wait_ge(out_lo, OUT_LO[l][2] + 1)
                        transpose_head(q0 + nt, i0 + item, False)
                        t_of[h] = q0 + nt
                        nt += 1
                    elif k == "V":
                        h = ev[1]
                        g = h // 4
                        par = g % 2
                        if h % 4 == 0:
                            if g:
                                pe.wait_ge(proj_out, p0 + 3 * (g - 1) + 3)
                            if g == 2:
                                pe.wait_ge(out_lo, OUT_LO[l][0] + 1)
                            if g == 3:
                                pe.wait_ge(exped, i0 + 20)
                        if g == 2:
                            pe.wait_ge(pt_ready, t_of[h] + 1)
                            p = pt[:, (hd0 + h) % 4, :]
                            for qt in range(2):
                                for kt in range(2):
                                    mm = pe.matmul(bank[6][:, qt * T + (h % 4) * HD:qt * T + (h % 4 + 1) * HD],
                                                   p[:, kt * T + qt * P:kt * T + (qt + 1) * P],
                                                   vg[:, par, kt, (h % 4) * HD:(h % 4 + 1) * HD], start=(kt == 0), stop=(kt == 1))
                            mm.then_inc(pv_done, 1)
                        else:
                            head_out(hd0 + h, t_of[h], h % 4, [6, 7, None, 0][g], vg[:, par], False)
                    elif k == "diff_T":
                        pe.wait_ge(d_n, l + 1)
                        q = q0 + nt
                        pe.wait_ge(pt_ready, q - 1)
                        for cc in range(2):
                            for qt in range(2):
                                mm = pe.transpose(bank[2 + q % 2][:, cc * T + qt * P:cc * T + (qt + 1) * P],
                                                  dno[:, qt * T + cc * P:qt * T + (cc + 1) * P], ident[:, :])
                        mm.then_inc(transposed, 1)
                        nt += 1

            mix(0)
            ffn(2)
            mix(1)
            ffn(3)


_INS = ["x", "norm_mixer", "norm_ffn", "pool_w", "pool_scale", "kv_norm", "w_kv", "w_q", "w_o", "rel_bias",
        "w_gate_up", "w_down", "final_norm", "attn_norm_2", "w_in_2", "na_rpb_2", "diff_lambda_2",
        "diff_subln_2", "mla_q_norm_2", "w_uq_2", "mla_kv_norm_2", "w_ukv_2", "t5_table_2", "w_o_2",
        "ffn_norm_2", "w_gate_2", "w_up_2", "w_down_2", "final_norm_2"]


def kernel(**inputs):
    import concourse.bacc as bacc
    from concourse.bass_utils import run_bass_kernel_spmd

    nc = bacc.Bacc("TRN2", target_bir_lowering=False, num_devices=1)
    arrays, a, c = {}, {}, {}
    for name in _INS:
        v = np.asarray(inputs[name])
        if name == "na_rpb_2":
            v = v[:, :, ::-1, ::-1]
        v = np.ascontiguousarray(v)
        arrays["in_" + name] = v
        a[name] = nc.dram_tensor("in_" + name, v.shape, F32, kind="ExternalInput").ap()
    for name, v in shape_constants().items():
        v = np.ascontiguousarray(v)
        arrays["in_" + name] = v
        c[name] = nc.dram_tensor("in_" + name, v.shape, F32, kind="ExternalInput").ap()
    out = nc.dram_tensor("result", (1, T, D), F32, kind="ExternalOutput").ap()
    bass_two_stacks(nc, a, c, out)
    r = run_bass_kernel_spmd(nc, [arrays], core_ids=[0])
    return r.results[0]["result"]
```

```python
import math
from contextlib import ExitStack

import numpy as np

import concourse.bass as bass
from concourse import mybir

F32 = mybir.dt.float32
F32R = mybir.dt.float32r
ALU = mybir.AluOpType
ACT = mybir.ActivationFunctionType
AX_X = mybir.AxisListType.X

P = 128
T = 256
D = 1024
TT = T // P
KC = D // P
HALF = 512
DFF = 2816
FB = 256
NB = DFF // FB
FFN_UNITS = 3 * NB
UNIT = 2048
SLOTS = 3
EPS = 1e-6
NEG = -1e30
BIG = 3.0e38
HD = 64
NBUCKET = 32
SEQ_D = 2 * T
MLA_QR, MLA_KVR, ROPE = 256, 128, 32
MLA_D = HD + ROPE
IN_W = 2720

POOL_U = 0
FFN_U = [1, 50, 98, 146]
MOBA_U = 34
MIX_U = [83, 131]
N_UNITS = 179


def _bucket_moba(n):
    exact = NBUCKET // 2
    nf = np.maximum(n, exact).astype(np.float32)
    large = exact + (np.log(nf / np.float32(exact)) / np.float32(math.log(128 / exact))
                     * np.float32(NBUCKET - exact)).astype(np.int32)
    return np.where(n < exact, n, np.minimum(large, NBUCKET - 1))


def _bucket_t5(rel):
    nb = NBUCKET // 2
    exact = nb // 2
    n = np.abs(rel)
    large = exact + (np.log(np.maximum(n, 1).astype(np.float32) / np.float32(exact))
                     / np.float32(math.log(1024 / exact)) * np.float32(nb - exact)).astype(np.int32)
    return np.where(rel > 0, nb, 0) + np.where(n < exact, n, np.minimum(large, nb - 1))


def shape_constants():
    f = np.float32
    out = {}
    out["c_ident"] = np.eye(P, dtype=f)
    t = np.arange(T)
    band = np.zeros((4, T, T), f)
    for g, win in enumerate((2, 4, 8, 16)):
        start = np.maximum(t + 1 - win, 0)
        s = t[:, None]
        inside = (s <= t[None, :]) & (s >= start[None, :])
        band[g] = np.where(inside, (f(1) / (t + 1 - start).astype(f))[None, :], f(0)) - np.eye(T, dtype=f)
    out["c_band"] = band
    d = np.arange(-(T - 1), T)
    moba = np.zeros((NBUCKET + 1, SEQ_D), f)
    past = d <= 0
    moba[_bucket_moba(np.maximum(-d, 0))[past], np.arange(d.size)[past]] = 1
    moba[NBUCKET, :d.size] = np.where(past, 0, NEG)
    moba[:, :d.size] = moba[:, :d.size][:, ::-1].copy()
    out["c_moba"] = moba
    t5 = np.zeros((2, NBUCKET + 1, SEQ_D), f)
    t5[:, _bucket_t5(d), np.arange(d.size)] = 1
    count = sum(((np.abs(d) <= (w // (2 * r)) * r) & (d % r == 0)).astype(int)
                for w, r in ((128, 1), (512, 4), (2048, 16)))
    t5[1, NBUCKET, :d.size] = np.where(count > 0, np.log(np.maximum(count, 1)), NEG)
    t5[:, :, :d.size] = t5[:, :, :d.size][:, :, ::-1].copy()
    out["c_t5"] = t5
    c = np.arange(64)
    first = np.clip(c - 8, 0, 48)[:, None]
    inside = (c[None, :] >= first) & (c[None, :] < first + 16)
    out["c_nmask"] = np.tile(np.where(inside, 0, NEG).astype(f)[:, ::-1], (2, 1))
    half = ROPE // 2
    inv = f(10000.0) ** (-np.arange(half, dtype=f) / f(half))
    ang = t.astype(f)[:, None] * inv[None, :]
    cos, sin = np.cos(ang).T, np.sin(ang).T
    k = np.concatenate([cos, cos, -sin, sin]).astype(f)
    out["c_rope"] = np.stack([(k * f(MLA_D ** -0.5)).astype(f), k], axis=1)
    return out


def moba_script():
    s = [("q_norm",)]
    def unit(n):
        return [("unit", n), ("split", n + 2), ("proj", n)]
    s += unit(0) + [("kv_norm",)] + unit(1) + [("kv_h",)]
    for n in range(2, 6):
        s += unit(n)
    def S(*x):
        return [("S", i) for i in x] + [("N", i) for i in x]
    def TH(*x):
        return [("T", i) for i in x]
    for g in range(4):
        i = 4 * g
        s += S(i, i + 1) + unit(6 + 2 * g)
        s += TH(i, i + 1) + S(i + 2, i + 3) + unit(7 + 2 * g)
        s += TH(i + 2, i + 3) + [("V", i + h) for h in range(4)] + [("O", g)]
    s += unit(14) + [("unit", 15), ("split", 17)]
    return s


def mix_script():
    s = []
    def unit(n):
        return [("unit", n), ("split", n + 2), ("proj", n)]
    def S(*x):
        return [("S", i) for i in x]
    def N(*x):
        return [("N", i) for i in x]
    def TH(*x):
        return [("T", i) for i in x]
    def V(*x):
        return [("V", i) for i in x]
    s += unit(0) + unit(1) + unit(2) + [("mla_T",)] + unit(3) + [("mla_B",), ("mla_G",)] + unit(4)
    s += S(0, 1) + N(0, 1) + unit(5)
    s += TH(0, 1) + S(2, 3) + N(2, 3) + unit(6)
    s += TH(2, 3) + S(4, 5) + N(4, 5) + V(0, 1, 2, 3) + [("O", 0)] + S(6, 7) + N(6, 7) + unit(7)
    s += TH(4, 5) + S(8, 9) + N(8, 9) + TH(6, 7) + V(4, 5) + S(10, 11) + N(10, 11) + unit(8)
    s += TH(8, 9) + S(12, 13) + N(12, 13) + V(6, 7) + [("O", 1)] + V(8, 9) + S(14, 15) + N(14, 15) + unit(9)
    s += TH(10, 11) + V(10, 11) + [("diff_stats",)] + S(16, 17) + N(16, 17) + [("diff_norm",)] + unit(10)
    s += [("diff_T",)] + S(18, 19) + N(18, 19) + TH(12) + unit(11)
    s += TH(13, 14) + V(12, 13) + TH(15) + unit(12)
    s += V(14, 15) + [("O", 3)] + unit(13) + [("unit", 14), ("split", 16)]
    return s


def bass_two_stacks(nc, a, c, out):
    ctx = ExitStack()
    with ctx:
        def sb(name, shape, dt=F32):
            return ctx.enter_context(nc.sbuf_tensor(name, shape, dt))

        def sem(name):
            return ctx.enter_context(nc.semaphore(name))

        raw = sb("raw", [P, SLOTS, UNIT])
        whi = sb("whi", [P, SLOTS, UNIT], F32R)
        wlo = sb("wlo", [P, SLOTS, UNIT], F32R)
        x = sb("x", [P, TT, D])
        xn = sb("xn", [P, TT, D])
        gains = sb("gains", [P, 2, D])
        h_hi = sb("h_hi", [P, KC, T], F32R)
        h_lo = sb("h_lo", [P, KC, T], F32R)
        o_hi = sb("o_hi", [P, KC, T], F32R)
        o_lo = sb("o_lo", [P, KC, T], F32R)
        qall = sb("qall", [P, KC, T])
        qg = sb("qg", [P, 2, 2, T])
        kg = sb("kg", [P, 2, 2, T])
        vg = sb("vg", [P, 2, TT, 4 * HD])
        bias = sb("bias", [P, 5120])
        pr = sb("pr", [P, 8, 2, T])
        pt = sb("pt", [P, 4, 2 * T])
        ident = sb("ident", [P, P])
        junk = sb("junk", [P, HALF], mybir.dt.bfloat16)
        ssq = sb("ssq", [P, TT, 2])
        msq = sb("msq", [P, 8])
        rstd = sb("rstd", [P, 8])
        neghalf = sb("neghalf", [P, 8])
        negmax = sb("negmax", [P, 8, 2])
        psumrow = sb("psumrow", [P, 8, 2])
        rsum = sb("rsum", [P, 8, 2])
        dsq = sb("dsq", [P, 8])
        dms = sb("dms", [P, 8])
        drs = sb("drs", [P, 8])
        msm = sb("msm", [P, 2])
        ones = sb("ones", [P, 1])
        tab_moba = sb("tab_moba", [NBUCKET + 1, 16])
        tab_t5 = sb("tab_t5", [NBUCKET + 1, 8])
        nmask = sb("nmask", [P, 64])
        rope = sb("rope", [P, 2, T])
        lam_in = sb("lam_in", [P, 2, P])
        lam_s = sb("lam_s", [P, 2, 2])
        lam_e = sb("lam_e", [P, 2, 2])
        neglam = sb("neglam", [P, 2])
        subln = sb("subln", [P, 2])
        subln_s = sb("subln_s", [P, 2])
        mlag = sb("mlag", [P, 2, 3])
        wuq = sb("wuq", [P, 2, 4, P])
        wukv = sb("wukv", [P, 4, 2, HD])

        band = qall[:, :, :].rearrange("p (g s) t -> p g s t", g=4)
        vecs = pr[:, 0:3, :, :].rearrange("p i a b -> p i (a b)")
        onehots = pr[:, 3:6, :, :].rearrange("p i a b -> p i (a b)")
        rpb_pad = pr[:, 6, 0, 0:P]
        sil = pr[:, 0, :, :].rearrange("p a b -> p (a b)")
        act32 = pr[:, 1, :, :].rearrange("p a b -> p (a b)")
        def latq(t):
            return xn[:, 0, t * MLA_QR:(t + 1) * MLA_QR]

        kv_sq = xn[:, 0, 512:768]
        latT = xn[:, 1, 0:768].rearrange("p (c t) -> p c t", c=3)
        ropet = pt[:, 2:4, :]
        dno = xn[:, 0, 0:HALF]
        dsquare = xn[:, 0, HALF:D]
        bias_moba = bias[:, 0:16 * T].rearrange("p (h k) -> p h k", h=16)
        bias_diff = bias[:, 0:4 * 384].rearrange("p (h k) -> p h k", h=4)
        bias_dil = bias[:, 1536:3072].rearrange("p (h k) -> p h k", h=4)
        bias_na = bias[:, 3072:5120].rearrange("p (q h k) -> p q h k", q=2, h=4)

        bank = [ctx.enter_context(nc.psum_tensor(f"bank{i}", [P, HALF], F32)) for i in range(8)]
        ACC = [4, 5, 6, 7]

        vec_dram = nc.dram_tensor("vec_scratch", [24, SEQ_D], F32, kind="Internal")
        rpb_dram = nc.dram_tensor("rpb_scratch", [120, P], F32, kind="Internal")

        raw_in = [sem(f"raw_in{i}") for i in range(SLOTS)]
        hi_ready, lo_ready, units_used = sem("hi_ready"), sem("lo_ready"), sem("units_used")
        x_in = sem("x_in")
        small_in, scale_in, pool_scaled = sem("small_in"), sem("scale_in"), sem("pool_scaled")
        table_in, onehot_in = sem("table_in"), sem("onehot_in")
        layer_in = [sem("layer_in0"), sem("layer_in1")]
        gains_in = [sem("gains_in0"), sem("gains_in1")]
        band_in = sem("band_in")
        scratch_out, bias_in, bias2_in, na_in = sem("scratch_out"), sem("bias_in"), sem("bias2_in"), sem("na_in")
        na_ready = sem("na_ready")
        consts_set, pad_set, vec_done, vec_out = sem("consts_set"), sem("pad_set"), sem("vec_done"), sem("vec_out")
        x_ready, squares, msq_ready, rstd_ready = sem("x_ready"), sem("squares"), sem("msq_ready"), sem("rstd_ready")
        xn_ready, xT_ready, hT_hi, hT_lo = sem("xn_ready"), sem("xT_ready"), sem("hT_hi"), sem("hT_lo")
        acc_ready = sem("acc_ready")
        silu_ready, glu_ready, act_hi, act_ready = sem("silu_ready"), sem("glu_ready"), sem("act_hi"), sem("act_ready")
        proj_out = sem("proj_out")
        scores, maxed, exped, normed = sem("scores"), sem("maxed"), sem("exped"), sem("normed")
        transposed, pt_ready, pv_done = sem("transposed"), sem("pt_ready"), sem("pv_done")
        out_hi, out_lo = sem("out_hi"), sem("out_lo")
        mla_sq, mla_ms, mla_rs, mla_lat, mla_t, mla_tT = (sem("mla_sq"), sem("mla_ms"), sem("mla_rs"),
                                                          sem("mla_lat"), sem("mla_t"), sem("mla_tT"))
        kv_sum, kv_mean, kv_rsqrt, kv_bcast, kv_lat = sem("kv_sum"), sem("kv_mean"), sem("kv_rsqrt"), sem("kv_bcast"), sem("kv_lat")
        mla_g, mla_rope, mla_copied = sem("mla_g"), sem("mla_rope"), sem("mla_copied")
        d_sq, d_red, d_ms, d_rs, d_n = sem("d_sq"), sem("d_red"), sem("d_ms"), sem("d_rs"), sem("d_n")
        lam_r, lam_x, lam_done, vchain = sem("lam_r"), sem("lam_x"), sem("lam_done"), sem("vchain")
        pool_d, rpb_in, ones_set = sem("pool_d"), sem("rpb_in"), sem("ones_set")
        fin, stored = sem("fin"), sem("stored")

        NORM_X = {0: 0, 1: 1, 2: 2, 3: 2, 4: 3, 5: 4, 6: 5, 7: 6, 8: 7, 9: 8, 10: 9}
        XN_NO = {0: 0, 1: 1, 2: 2, 3: 3, 4: 4, 6: 5, 7: 6, 8: 7, 9: 8}
        HT_NO = {0: 0, 1: 1, 2: 2, 3: 3, 4: 4, 6: 5, 7: 6, 8: 7, 9: 8}
        ACC_NO = {1: 0, 2: 1, 3: 2, 4: 3, 6: 4, 7: 5, 8: 6, 9: 7}
        GAIN_SRC = {0: a["norm_mixer"][0], 1: a["norm_ffn"][0], 2: a["norm_mixer"][1], 3: a["kv_norm"],
                    4: a["norm_ffn"][1], 5: a["final_norm"], 6: a["attn_norm_2"][0], 7: a["ffn_norm_2"][0],
                    8: a["attn_norm_2"][1], 9: a["ffn_norm_2"][1], 10: a["final_norm_2"]}

        LAST_U = {1: POOL_U, 2: FFN_U[0] + 32, 3: MOBA_U + 15, 4: FFN_U[1] + 32, 6: MIX_U[0] + 14,
                  7: FFN_U[2] + 32, 8: MIX_U[1] + 14, 9: FFN_U[3] + 32}
        AFTER_FFN = (2, 4, 7, 9)

        def tile_no(v, t):
            return 8 + 2 * t + (v - 4) if v in (4, 5) else 2 * v + t

        def part_no(v, t, h):
            return 2 * tile_no(v, t) + h

        OUT_HI = [{0: 4, 1: 5, 3: 6}, {0: 7, 1: 8, 3: 9}]
        OUT_LO = [[4, 5, 6, 7], [8, 9, 10, 11]]
        T_DIFF = 12

        def stage_items(layer):
            return 16 + 20 * layer, 16 + 17 * layer, 12 + 9 * layer

        def item_of_head(h):
            return h if h < 8 else 8 + 2 * (h - 8) if h < 12 else h + 4

        T_BEFORE = {}
        freed = {i: i + 1 for i in range(16)}
        for l in range(2):
            i0, q0, _ = stage_items(l)
            nt = 0
            for ev in mix_script():
                if ev[0] == "T":
                    first = item_of_head(ev[1])
                    for i in range(first, first + (2 if 8 <= ev[1] < 12 else 1)):
                        freed[i0 + i] = q0 + nt + 1
                if ev[0] in ("T", "diff_T"):
                    nt += 1
        for i in range(8, 56):
            T_BEFORE[i] = freed[i - 8]

        def down_from(tile, start, n):
            ap = tile[:, 0:n]
            return bass.AP(ap.tensor, ap.offset + start, [list(ap.ap[0]), [-1, n]])

        def mix_bank(n):
            return (6 if n in (2, 3) else 4) + n % 2

        def kr_parts(dst, src):
            d = dst[:, 0:KC * 192].rearrange("p (k n) -> p k n", k=KC)
            s = src[:, 0:KC * 160].rearrange("p (k n) -> p k n", k=KC)
            return [(d[:, :, 0:160], s[:, :, 0:160]), (d[:, :, 160:176], s[:, :, 144:160]),
                    (d[:, :, 176:192], s[:, :, 128:144])]

        def slot_of(n):
            return n % SLOTS

        def k8(w, c0, width=FB):
            return w[:, bass.ds(c0, width)].rearrange("(k p) n -> p k n", p=P)

        def k2(w, r0):
            return w[bass.ds(r0, 2 * P), :].rearrange("(k p) n -> p k n", p=P)

        def ffn_weights(f):
            if f < 2:
                gu = a["w_gate_up"][f]
                return gu[:, 0:DFF], gu[:, DFF:2 * DFF], a["w_down"][f]
            return a["w_gate_2"][f - 2], a["w_up_2"][f - 2], a["w_down_2"][f - 2]

        W_IN_COLS = [2304, 2560, 256, 0, 512, 1024, 768, 1280, 1792, 1536, 2048]
        MIX_O_ROWS = [768, 0, 256, 512]
        MIX_OUT_CHUNK = [6, 0, 2, 4]

        def moba_src(n):
            if n < 4:
                return k8(a["w_q"][0], 256 * n)
            if n < 12:
                g = (n - 4) // 2
                return k8(a["w_kv"], 256 * g + (D if n % 2 else 0))
            return k2(a["w_o"][0], 256 * (n - 12))

        def mix_src(layer, n):
            if n == 1:
                return k8(a["w_in_2"][layer], 2560, 160)
            if n < 11:
                return k8(a["w_in_2"][layer], W_IN_COLS[n])
            return k2(a["w_o_2"][layer], MIX_O_ROWS[n - 11])

        block = ctx.enter_context(nc.Block())

        @block.sync
        def _(sp):
            def load(src, n, b=0, slot=None):
                if not (isinstance(n, int) and n < SLOTS and isinstance(b, int)):
                    sp.wait_ge(lo_ready, n - 2 + 3 * b)
                s = slot_of(n)
                dst = raw[:, s, :]
                if tuple(src.shape)[1:] == (KC, 160):
                    dst = raw[:, s, 0:KC * 160]
                dst = dst.rearrange("p (k n) -> p k n", k=src.shape[1])
                sp.dma_start(dst, src).then_inc(raw_in[s], 16)

            def load_gain(j):
                if j >= 2:
                    prev = j - 2
                    if prev == 5:
                        sp.wait_ge(x_ready, 4 * 5)
                    else:
                        sp.wait_ge(xn_ready, 4 * XN_NO[prev] + 4)
                sp.dma_start(gains[:, j % 2, :], GAIN_SRC[j].unsqueeze(0).broadcast_to([P, D])).then_inc(gains_in[j % 2], 16)

            xv = a["x"].rearrange("a (t p) d -> (a t) p d", p=P)
            for t in range(TT):
                sp.dma_start(x[:, t, :], xv[t]).then_inc(x_in, 16)
            load_gain(0)
            sp.dma_start(tab_moba[0:NBUCKET, :], a["rel_bias"]).then_inc(table_in, 16)
            sp.dma_start(tab_t5[0:NBUCKET, :], a["t5_table_2"]).then_inc(table_in, 16)
            sp.dma_start(onehots[0:NBUCKET + 1, 0, :], c["c_moba"]).then_inc(onehot_in, 16)
            for i in range(2):
                sp.dma_start(onehots[0:NBUCKET + 1, 1 + i, :], c["c_t5"][i]).then_inc(onehot_in, 16)
            sp.dma_start(band, c["c_band"].rearrange("g (s p) t -> p g s t", p=P)).then_inc(band_in, 16)
            sp.dma_start(pt[:, 0:2, :].rearrange("p a b -> p (a b)"), a["pool_scale"].broadcast_to([P, D])).then_inc(scale_in, 16)
            sp.dma_start(raw[:, 0, :].rearrange("p (g k n) -> p (g k) n", g=4, k=2),
                         a["pool_w"].rearrange("a g (k p) n -> p (a g k) n", p=P)).then_inc(raw_in[0], 16)
            load(k8(ffn_weights(0)[0], 0), FFN_U[0])
            sp.dma_start(ident[:, :], c["c_ident"]).then_inc(small_in, 16)
            load_gain(1)
            sp.dma_start(nmask[:, :], c["c_nmask"]).then_inc(small_in, 16)
            sp.dma_start(rope[64:128, :, :], c["c_rope"]).then_inc(small_in, 16)
            for l in range(2):
                lam = a["diff_lambda_2"][l].rearrange("a b -> (a b)")
                sp.dma_start(lam_in[:, l, :], lam.unsqueeze(0).broadcast_to([P, P])).then_inc(small_in, 16)
                for r in range(2):
                    sp.dma_start(subln[64 * r:64 * r + 64, l:l + 1], a["diff_subln_2"][l].unsqueeze(1)).then_inc(small_in, 16)
                for k in range(2):
                    sp.dma_start(mlag[:, l, k:k + 1], a["mla_q_norm_2"][l, k * P:(k + 1) * P].unsqueeze(1)).then_inc(small_in, 16)
                sp.dma_start(mlag[:, l, 2:3], a["mla_kv_norm_2"][l].unsqueeze(1)).then_inc(small_in, 16)
            sp.wait_ge(pad_set, 1)
            sp.dma_start(rpb_pad[0:120, 48:79], a["na_rpb_2"].rearrange("l h r c -> (l h r) c")).then_inc(rpb_in, 16)

            def load_layer(l):
                if l:
                    sp.wait_ge(mla_g, 3)
                u = a["w_uq_2"][l].rearrange("(k p) (h n) -> p k h n", p=P, h=4)
                for k in range(2):
                    for lo, hi, at in ((0, MLA_D, 0), (80, 96, 96), (64, 80, 112)):
                        sp.dma_start(wuq[:, k, :, at:at + hi - lo], u[:, k, :, lo:hi]).then_inc(layer_in[l], 16)
                sp.dma_start(wukv[:, :, :, :].rearrange("p h a n -> p (h a n)"), a["w_ukv_2"][l]).then_inc(layer_in[l], 16)

            def ffn(f):
                u0 = FFN_U[f]
                wg, wu, wd = ffn_weights(f)
                if f:
                    load(k8(wg, 0), u0)
                load(k8(wu, 0), u0 + 1)
                yield
                load(k8(wg, FB), u0 + 2)
                load(k8(wu, FB), u0 + 3)
                load(k2(wd, 0), u0 + 4)
                yield
                with sp.Fori(2, NB - 1) as b:
                    load(k8(wg, b * FB), u0 - 1, b)
                    load(k8(wu, b * FB), u0, b)
                    load(k2(wd, (b - 1) * FB), u0 + 1, b)
                n = u0 + 3 * (NB - 1)
                load(k8(wg, (NB - 1) * FB), n - 1)
                load(k8(wu, (NB - 1) * FB), n)
                load(k2(wd, (NB - 2) * FB), n + 1)
                load(k2(wd, (NB - 1) * FB), n + 2)
                yield

            stage = ffn(0)
            next(stage)
            sp.wait_ge(vec_out, 3)
            for r0, nr, i in ((0, 16, 0), (16, 4, 1), (20, 4, 2)):
                sp.dma_start(vec_dram.ap()[r0:r0 + nr, :], vecs[0:nr, i, :]).then_inc(scratch_out, 16)
            sp.wait_ge(rpb_in, 16)
            sp.dma_start(rpb_dram.ap(), rpb_pad[0:120, :]).then_inc(scratch_out, 16)
            next(stage)
            load_gain(2)
            load_gain(3)
            next(stage)

            for n in range(16):
                load(moba_src(n), MOBA_U + n)
                if n == 1:
                    sp.wait_ge(scratch_out, 64)
                    sp.dma_start(bias_moba, bass.AP(vec_dram, P, [[1, P], [SEQ_D, 16], [1, T]])).then_inc(bias_in, 16)
                if n == 5:
                    load_gain(4)
                    load_gain(5)

            def load_na(l, r):
                for h in range(4):
                    off = ((l * 4 + h) * 15 + 4 + r) * P
                    sp.dma_start(bias_na[64 * (r % 2):64 * (r % 2) + 64, r // 2, h, :].rearrange("p (a b) -> p a b", a=4),
                                 bass.AP(rpb_dram, off, [[1, 64], [P, 4], [1, 64]])).then_inc(na_in, 16)

            stage = ffn(1)
            next(stage)
            next(stage)
            load_gain(6)
            next(stage)
            for l in range(2):
                for n in range(15):
                    load(mix_src(l, n), MIX_U[l] + n)
                    if n == 0:
                        load_layer(l)
                    if 1 <= n < 5:
                        if n == 1:
                            sp.wait_ge(*((exped, 16 + 8) if l else (normed, 16)))
                        load_na(l, n - 1)
                    if n == 5 and l == 0:
                        for i, dst in ((0, bias_diff), (1, bias_dil)):
                            sp.dma_start(dst, bass.AP(vec_dram, (16 + 4 * i) * SEQ_D, [[1, P], [SEQ_D, 4], [1, 384]])).then_inc(bias2_in, 16)
                    if n == 7:
                        load_gain(7 if l == 0 else 10)
                    if n == 9 and l == 0:
                        load_gain(8)
                if l == 0:
                    stage = ffn(2)
                    next(stage)
                    next(stage)
                    load_gain(9)
                    next(stage)
            for _step in ffn(3):
                pass
            ov = out.rearrange("a (t p) d -> (a t) p d", p=P)
            for t in range(TT):
                for h in range(2):
                    sp.wait_ge(fin, 2 * t + h + 1)
                    sp.dma_start(ov[t][:, h * HALF:(h + 1) * HALF], xn[:, t, h * HALF:(h + 1) * HALF]).then_inc(stored, 16)
            sp.wait_ge(stored, 64)

        @block.gpsimd
        def _(pool):
            pool.memset(neghalf[:, :], -0.5).then_inc(consts_set, 1)
            pool.memset(ones[:, :], 1.0).then_inc(consts_set, 1)
            pool.wait_ge(consts_set, 2)
            pool.memset(rpb_pad, 0.0).then_inc(pad_set, 1)

            def rsqrt(version):
                for t in range(TT):
                    rsqrt_tile(version, t)

            def rsqrt_tile(version, t):
                pool.wait_ge(msq_ready, tile_no(version, t) + 1)
                pool.tensor_tensor(rstd[:, t:t + 1], msq[:, t:t + 1], neghalf[:, 0:1], ALU.pow).then_inc(rstd_ready, 1)

            def mask_na(l):
                pool.wait_ge(na_in, 256 * (l + 1))
                if l == 0:
                    pool.wait_ge(small_in, 15 * 16)
                for q in range(2):
                    for h in range(4):
                        v = bias_na[:, q, h, :].rearrange("p (a b) -> p a b", a=4)
                        pool.tensor_tensor(v, v, nmask[:, :].unsqueeze(1).broadcast_to([P, 4, 64]), ALU.add).then_inc(na_ready, 1)

            def mix(l):
                pool.wait_ge(mla_ms, l + 1)
                pool.tensor_tensor(rstd[:, 2:4], msq[:, 2:4], neghalf[:, 0:2], ALU.pow).then_inc(mla_rs, 1)
                pool.wait_ge(kv_mean, l + 1)
                pool.tensor_tensor(rstd[:, 4:6], msq[:, 4:6], neghalf[:, 0:2], ALU.pow).then_inc(kv_rsqrt, 1)
                mask_na(l)
                pool.wait_ge(d_ms, l + 1)
                pool.tensor_tensor(drs[:, :], dms[:, :], neghalf[:, :], ALU.pow).then_inc(d_rs, 1)

            for v in range(4):
                rsqrt(v)
            for t in range(TT):
                for v in (4, 5):
                    rsqrt_tile(v, t)
            mix(0)
            rsqrt(6)
            rsqrt(7)
            mix(1)
            rsqrt(8)
            rsqrt(9)

        @block.scalar
        def _(act):
            def split(n, b=0):
                s = slot_of(n)
                if n == POOL_U:
                    act.wait_ge(pool_scaled, 1)
                else:
                    act.wait_ge(raw_in[s], 16 * (n // SLOTS + 1 + b))
                if not (isinstance(b, int) and n + 3 * b < SLOTS):
                    act.wait_ge(units_used, n - 2 + 3 * b)
                if n in (MIX_U[0] + 1, MIX_U[1] + 1):
                    for dst, src in kr_parts(whi[:, s, :], raw[:, s, :]):
                        i = act.activation(dst, src, ACT.Copy)
                    i.then_inc(hi_ready, 1)
                else:
                    act.activation(whi[:, s, :], raw[:, s, :], ACT.Copy).then_inc(hi_ready, 1)

            def square(version, t, h):
                if version:
                    act.wait_ge(x_ready, part_no(version, t, h) - 3)
                    act.wait_ge(msq_ready, tile_no(version - 1, t) + 1)
                else:
                    act.wait_ge(x_in, 32)
                if version or t or h:
                    act.wait_ge(squares, part_no(version, t, h))
                act.activation(junk[:, :], x[:, t, h * HALF:(h + 1) * HALF], ACT.Square, scale=1.0 / 32,
                               accum_out=ssq[:, t, h:h + 1]).then_inc(squares, 1)

            def h_out(j, t, h):
                dst = o_hi if j == 2 else h_hi
                act.wait_ge(xT_ready, 4 * (HT_NO[j] - 1) + 2 * t + h + 1)
                act.activation(dst[:, 4 * h:4 * h + 4, t * P:(t + 1) * P],
                               bank[2 * t + h][:, :].rearrange("p (c k) -> p c k", c=4), ACT.Copy).then_inc(hT_hi, 1)

            def norm(j, square_too=True, late_split=None):
                for t in range(TT):
                    for h in range(2):
                        if square_too:
                            square(NORM_X[j], t, h)
                    if t == 0 and late_split is not None:
                        split(late_split)
                        for h in range(2):
                            h_out(j, 0, h)
                for t in range(0 if late_split is None else 1, TT):
                    for h in range(2):
                        h_out(j, t, h)

            def ffn(f):
                u0, e0 = FFN_U[f], NB * f
                norm([1, 4, 7, 9][f])
                if f == 0:
                    for l in range(2):
                        act.wait_ge(lam_r, 2 * l + 2)
                        act.activation(lam_e[:, l, :], lam_s[:, l, :], ACT.Exp).then_inc(lam_x, 1)

                def silu(b, par):
                    act.wait_ge(units_used, u0 + 3 * b)
                    act.wait_ge(glu_ready, e0 + b)
                    act.activation(sil, bank[2 * par][:, :], ACT.Silu).then_inc(silu_ready, 1)

                split(u0 + 2)
                split(u0 + 3)
                act.wait_ge(units_used, u0 + 1)
                if e0:
                    act.wait_ge(glu_ready, e0)
                else:
                    act.wait_ge(scratch_out, 64)
                act.activation(sil, bank[ACC[0]][:, :], ACT.Silu).then_inc(silu_ready, 1)

                def block_steps(b, par):
                    for k in (1, 2, 3):
                        split(u0 + k, b)
                    silu(b, par)

                block_steps(1, 1)
                with act.Fori(2, NB - 1, 2) as b:
                    block_steps(b, 0)
                    block_steps(b + 1, 1)
                n = u0 + 3 * (NB - 1)
                split(n + 1)
                split(n + 2)
                silu(NB - 1, 0)
                if n + 3 < N_UNITS:
                    split(n + 3)

            def proj_copy(no, n, dst, bk, scale=1.0):
                act.wait_ge(units_used, n + 1)
                act.activation(dst, bk, ACT.Copy, scale=scale).then_inc(proj_out, 1)

            def exps(i, item, biased, width0=T):
                act.wait_ge(maxed, i + 1)
                s = i % 8
                for q in range(2):
                    w = width0 if q == 0 else T
                    src = pr[:, s, q, 0:w] if biased else bank[i % 2][:, q * T:q * T + w]
                    e = act.activation(pr[:, s, q, 0:w], src, ACT.Exp, bias=negmax[:, s, q:q + 1],
                                       scale=-1.0 if biased else 1.0, accum_out=psumrow[:, s, q:q + 1])
                e.then_inc(exped, 1)

            def pt_copy(q, head, width):
                act.wait_ge(transposed, q + 1)
                if head >= 4:
                    act.wait_ge(pv_done, head - 3)
                act.activation(pt[:, head % 4, 0:width], bank[2 + q % 2][:, 0:width], ACT.Copy).then_inc(pt_ready, 1)

            def o_copy(no, nheads, bk, chunk):
                act.wait_ge(pv_done, nheads)
                act.activation(o_hi[:, chunk:chunk + 2, :], bank[bk][:, :].rearrange("p (c k) -> p c k", c=2),
                               ACT.Copy).then_inc(out_hi, 1)

            for t in range(TT):
                for h in range(2):
                    square(0, t, h)
            for i, nr in enumerate((16, 4, 4)):
                act.wait_ge(vec_done, i + 1)
                act.activation(vecs[0:nr, i, 0:SEQ_D], bank[4 + i][0:nr, :], ACT.Copy).then_inc(vec_out, 1)
            for k in range(4):
                if k == 1:
                    split(0)
                    split(1)
                act.wait_ge(pool_d, k + 1)
                act.activation(h_hi[:, 2 * k:2 * k + 2, :], bank[k][:, :].rearrange("p (c k) -> p c k", c=2),
                               ACT.Copy).then_inc(hT_hi, 1)
            split(2)
            ffn(0)

            for ev in moba_script():
                k = ev[0]
                if k == "q_norm":
                    norm(2, late_split=MOBA_U + 1)
                elif k == "kv_h":
                    norm(3, False)
                elif k == "split":
                    split(MOBA_U + ev[1])
                elif k == "proj" and ev[1] < 12:
                    n = ev[1]
                    par = ((n - 4) // 2) % 2
                    bk = bank[4 + n % 2]
                    if n < 4:
                        proj_copy(n, MOBA_U + n, qall[:, 2 * n:2 * n + 2, :].rearrange("p a b -> p (a b)"), bk[:, :], HD ** -0.5)
                    elif n % 2 == 0:
                        if n >= 8:
                            act.wait_ge(scores, 4 * ((n - 4) // 2) - 4)
                        proj_copy(n, MOBA_U + n, kg[:, par].rearrange("p a b -> p (a b)"), bk[:, :])
                    else:
                        if n >= 9:
                            act.wait_ge(pv_done, 4 * ((n - 4) // 2) - 4)
                        proj_copy(n, MOBA_U + n, vg[:, par].rearrange("p a b -> p (a b)"), bk[:, :])
                elif k == "S":
                    exps(ev[1], ev[1], True, P)
                elif k == "T":
                    pt_copy(ev[1], ev[1], 3 * P)
                elif k == "O":
                    g = ev[1]
                    o_copy(g, 4 * g + 4, 0 if g == 3 else 6 + g % 2, 2 * g)
            ffn(1)

            def mix(l):
                i0, q0, p0 = stage_items(l)
                hd0 = 16 + 16 * l
                u0 = MIX_U[l]
                if l == 0:
                    for t in range(TT):
                        for h in range(2):
                            square(4, t, h)
                        if t:
                            for h in range(2):
                                h_out(6, 0, h)
                        for h in range(2):
                            square(5, t, h)
                        if t == 0:
                            split(u0 + 1)
                    for h in range(2):
                        h_out(6, 1, h)
                else:
                    norm(8, late_split=u0 + 1)
                nt = 0
                for ev in mix_script():
                    k = ev[0]
                    if k == "split":
                        split(u0 + ev[1])
                    elif k == "proj":
                        n = ev[1]
                        bk = bank[mix_bank(n)]
                        if n == 0:
                            act.wait_ge(units_used, u0 + 1)
                            act.wait_ge(squares, 4 * NORM_X[6 + 2 * l] + 4)
                            for t in range(TT):
                                if l or t:
                                    act.wait_ge(mla_sq, 3 * l + t)
                                act.activation(junk[:, 0:MLA_QR], bk[:, t * T:t * T + MLA_QR], ACT.Square, scale=MLA_QR ** -0.5,
                                               accum_out=msm[:, t:t + 1]).then_inc(mla_sq, 1)
                        elif n == 1:
                            act.wait_ge(units_used, u0 + 2)
                            act.activation(kv_sq, bk[:, 0:T], ACT.Square, scale=MLA_KVR ** -0.5).then_inc(mla_sq, 1)
                        elif n < 11:
                            g, kind = (n - 2) // 3, (n - 2) % 3
                            par = (g + 1) % 2
                            dst = (kg, qg, vg)[kind][:, par].rearrange("p a b -> p (a b)")
                            scale = 1.0
                            if kind == 1:
                                scale = (ROPE if g == 1 else HD) ** -0.5
                            if kind < 2 and g == 2:
                                act.wait_ge(scores, i0 + 8)
                            if kind == 2 and g:
                                act.wait_ge(pv_done, hd0 + 4 * g)
                            proj_copy(n, u0 + n, dst, bk[:, :], scale)
                    elif k == "mla_T":
                        act.wait_ge(small_in, 15 * 16)
                        act.wait_ge(mla_t, l + 1)
                        for cc in range(2):
                            e = act.activation(latT[:, cc, :], bank[0][:, cc * T:(cc + 1) * T], ACT.Copy, scale=mlag[:, l, cc:cc + 1])
                        e.then_inc(mla_tT, 1)
                    elif k == "mla_G":
                        act.wait_ge(mla_g, 3 * l + 1)
                        for c2 in range(2):
                            act.activation(qall[0:HD, 2 * c2:2 * c2 + 2, :], bank[c2][0:HD, :].rearrange("p (c k) -> p c k", c=2),
                                           ACT.Copy, scale=MLA_D ** -0.5)
                        act.wait_ge(mla_g, 3 * l + 2)
                        for c2 in range(2):
                            act.activation(qall[0:HD, 4 + 2 * c2:6 + 2 * c2, :], bank[2 + c2][0:HD, :].rearrange("p (c k) -> p c k", c=2), ACT.Copy)
                        act.wait_ge(mla_g, 3 * l + 3)
                        act.activation(vg[:, 0].rearrange("p a b -> p (a b)"), bank[6][:, :], ACT.Copy).then_inc(mla_copied, 1)
                    elif k == "S":
                        exps(i0 + ev[1], ev[1], ev[1] >= 4)
                    elif k == "T":
                        pt_copy(q0 + nt, hd0 + ev[1], 2 * T)
                        nt += 1
                    elif k == "diff_stats":
                        act.wait_ge(pv_done, hd0 + 12)
                        act.activation(dsquare, bank[6][:, :], ACT.Square, scale=HD ** -0.5).then_inc(d_sq, 1)
                    elif k == "diff_T":
                        act.wait_ge(transposed, q0 + nt + 1)
                        act.wait_ge(lam_done, 2)
                        act.activation(o_hi[:, 2:4, :], bank[2 + (q0 + nt) % 2][:, :].rearrange("p (c k) -> p c k", c=2),
                                       ACT.Copy, scale=subln_s[:, l:l + 1]).then_inc(pt_ready, 1)
                        nt += 1
                    elif k == "O":
                        g = ev[1]
                        o_copy(OUT_HI[l][g], hd0 + 4 * g + 4, [6, 7, None, 0][g], MIX_OUT_CHUNK[g])

            mix(0)
            ffn(2)
            mix(1)
            ffn(3)
            for t in range(TT):
                for h in range(2):
                    square(9, t, h)

        @block.vector
        def _(dve):
            chained = [0]

            def then_wait(i):
                chained[0] += 1
                i.then_inc(vchain, 1)
                dve.wait_ge(vchain, chained[0])

            def split(n, b=0):
                s = slot_of(n)
                dve.wait_ge(hi_ready, n + 1 + 3 * b)
                if n in (MIX_U[0] + 1, MIX_U[1] + 1):
                    parts = zip(kr_parts(wlo[:, s, :], raw[:, s, :]), kr_parts(whi[:, s, :], raw[:, s, :]))
                    for (dst, src), (hi, _) in parts:
                        i = dve.tensor_tensor(dst, src, hi.bitcast(F32), ALU.subtract)
                    i.then_inc(lo_ready, 1)
                else:
                    dve.tensor_tensor(wlo[:, s, :], raw[:, s, :], whi[:, s, :].bitcast(F32), ALU.subtract).then_inc(lo_ready, 1)

            def add_residual(version, t, h):
                if (t, h) == (1, 1):
                    dve.wait_ge(units_used, LAST_U[version] + 1)
                else:
                    dve.wait_ge(acc_ready, 3 * ACC_NO[version] + 2 * t + h + 1)
                xs = x[:, t, h * HALF:(h + 1) * HALF]
                acc = bank[ACC[2 * t + h]][:, :]
                dve.tensor_tensor(xs, xs, acc, ALU.add).then_inc(x_ready, 1)

            def mean_square(version, t):
                dve.wait_ge(squares, part_no(version, t, 1) + 1)
                if version:
                    dve.wait_ge(rstd_ready, tile_no(version - 1, t) + 1)
                dve.tensor_scalar(msq[:, t:t + 1], ssq[:, t, 0:1], ssq[:, t, 1:2], EPS, ALU.add, ALU.add).then_inc(msq_ready, 1)

            def normalise(j, t, h):
                if (t, h) == (0, 0):
                    dve.wait_ge(gains_in[j % 2], 16 * (j // 2 + 1))
                dve.wait_ge(rstd_ready, tile_no(NORM_X[j], t) + 1)
                if j in XN_NO and XN_NO[j] > 1:
                    dve.wait_ge(xT_ready, 4 * (HT_NO[j] - 2) + 2 * t + 2)
                cols = slice(h * HALF, (h + 1) * HALF)
                dst = x if j == 5 else xn
                done = x_ready if j == 5 else fin if j == 10 else xn_ready
                dve.scalar_tensor_tensor(out=dst[:, t, cols], in0=x[:, t, cols], scalar=rstd[:, t:t + 1],
                                         in1=gains[:, j % 2, cols], op0=ALU.mult, op1=ALU.mult).then_inc(done, 1)

            def h_lo_out(j, t, h):
                dst, hi = (o_lo, o_hi) if j == 2 else (h_lo, h_hi)
                dve.wait_ge(hT_hi, 4 * HT_NO[j] + 2 * t + h + 1)
                cols = (slice(None), slice(4 * h, 4 * h + 4), slice(t * P, (t + 1) * P))
                dve.tensor_tensor(dst[cols], bank[2 * t + h][:, :].rearrange("p (c k) -> p c k", c=4),
                                  hi[cols].bitcast(F32), ALU.subtract).then_inc(hT_lo, 1)

            def norm(j):
                v = NORM_X[j]
                add_residual(v, 0, 0)
                add_residual(v, 0, 1)
                mean_square(v, 0)
                if v in AFTER_FFN:
                    normalise(j, 0, 0)
                    normalise(j, 0, 1)
                    add_residual(v, 1, 0)
                    h_lo_out(j, 0, 0)
                    add_residual(v, 1, 1)
                    h_lo_out(j, 0, 1)
                    mean_square(v, 1)
                else:
                    add_residual(v, 1, 0)
                    add_residual(v, 1, 1)
                    normalise(j, 0, 0)
                    mean_square(v, 1)
                    normalise(j, 0, 1)
                normalise(j, 1, 0)
                normalise(j, 1, 1)
                for t in range(1 if v in AFTER_FFN else 0, TT):
                    for h in range(2):
                        h_lo_out(j, t, h)

            def lambdas():
                dve.wait_ge(small_in, 15 * 16)
                for l in range(2):
                    for r in range(2):
                        dve.tensor_tensor_reduce(lam_in[:, l, 64 * r:64 * r + 32], lam_in[:, l, 64 * r:64 * r + 32],
                                                 lam_in[:, l, 64 * r + 32:64 * r + 64], 1.0, 0.0, ALU.mult, ALU.add,
                                                 lam_s[:, l, r:r + 1]).then_inc(lam_r, 1)
                for l in range(2):
                    init = 0.8 - 0.6 * math.exp(-0.3 * l)
                    dve.wait_ge(lam_x, l + 1)
                    dve.tensor_scalar(neglam[:, l:l + 1], lam_e[:, l, 1:2], lam_e[:, l, 0:1], -init, ALU.subtract, ALU.add)
                    dve.tensor_scalar(subln_s[:, l:l + 1], subln[:, l:l + 1], 1.0 - init, None, ALU.mult).then_inc(lam_done, 1)
                dve.wait_ge(lam_done, 2)

            def ffn(f):
                u0, e0 = FFN_U[f], NB * f
                norm([1, 4, 7, 9][f])
                split(u0 + 1)
                if f == 0:
                    lambdas()

                def glu(b, par):
                    dve.wait_ge(silu_ready, e0 + b + 1)
                    if not (isinstance(b, int) and e0 + b == 0):
                        dve.wait_ge(act_ready, e0 + b)
                    dve.wait_ge(units_used, (u0 + 2 if isinstance(b, int) and b == 0 else u0 + 1 + 3 * b))
                    up = ACC[1] if isinstance(b, int) and b == 0 else 2 * par + 1
                    dve.tensor_tensor(act32, sil, bank[up][:, :], ALU.mult).then_inc(glu_ready, 1)
                    dve.wait_ge(glu_ready, e0 + b + 1)
                    hi = o_hi[:, 2 * par:2 * par + 2, :].rearrange("p a b -> p (a b)")
                    lo = o_lo[:, 2 * par:2 * par + 2, :].rearrange("p a b -> p (a b)")
                    if not isinstance(b, int) or b >= 2:
                        dve.wait_ge(units_used, u0 - 1 + 3 * b)
                    dve.tensor_copy(hi, act32).then_inc(act_hi, 1)
                    dve.wait_ge(act_hi, e0 + b + 1)
                    dve.tensor_tensor(lo, act32, hi.bitcast(F32), ALU.subtract).then_inc(act_ready, 1)

                split(u0 + 2)
                split(u0 + 3)
                glu(0, 0)

                def block_steps(b, par):
                    for k in (1, 2, 3):
                        split(u0 + k, b)
                    glu(b, par)

                block_steps(1, 1)
                with dve.Fori(2, NB - 1, 2) as b:
                    block_steps(b, 0)
                    block_steps(b + 1, 1)
                n = u0 + 3 * (NB - 1)
                split(n + 1)
                split(n + 2)
                glu(NB - 1, 0)
                if n + 3 < N_UNITS:
                    split(n + 3)

            def maxima(i, biases, width0=T):
                s = i % 8
                dve.wait_ge(scores, i + 1)
                if i >= 8:
                    dve.wait_ge(transposed, T_BEFORE[i])
                if biases is None:
                    dve.tensor_reduce(negmax[:, s, :], bank[i % 2][:, :].rearrange("p (q k) -> p q k", q=2), AX_X,
                                      ALU.max, negate=True).then_inc(maxed, 1)
                    return
                for q in range(2):
                    w = width0 if q == 0 else T
                    e = dve.tensor_tensor_reduce(pr[:, s, q, 0:w], bank[i % 2][:, q * T:q * T + w], biases[q], -1.0, BIG,
                                                 ALU.add, ALU.min, negmax[:, s, q:q + 1])
                e.then_inc(maxed, 1)

            def normal(i, width0=T, lam=None):
                s = i % 8
                dve.wait_ge(exped, i + 1)
                then_wait(dve.reciprocal(rsum[:, s, :], psumrow[:, s, :]))
                if lam is None:
                    for q in range(2):
                        w = width0 if q == 0 else T
                        e = dve.tensor_scalar(pr[:, s, q, 0:w], pr[:, s, q, 0:w], rsum[:, s, q:q + 1], None, ALU.mult)
                    e.then_inc(normed, 1)
                else:
                    then_wait(dve.tensor_scalar(rsum[:, s, :], rsum[:, s, :], lam, None, ALU.mult))
                    dve.wait_ge(normed, i)
                    for q in range(2):
                        e = dve.scalar_tensor_tensor(out=pr[:, s - 1, q, :], in0=pr[:, s, q, :], scalar=rsum[:, s, q:q + 1],
                                                     in1=pr[:, s - 1, q, :], op0=ALU.mult, op1=ALU.add)
                    e.then_inc(normed, 1)

            def o_low(no, bk, chunk):
                dve.wait_ge(out_hi, no + 1)
                dve.tensor_tensor(o_lo[:, chunk:chunk + 2, :], bank[bk][:, :].rearrange("p (c k) -> p c k", c=2),
                                  o_hi[:, chunk:chunk + 2, :].bitcast(F32), ALU.subtract).then_inc(out_lo, 1)

            dve.memset(tab_moba[NBUCKET:NBUCKET + 1, :], 1.0).then_inc(ones_set, 1)
            dve.memset(tab_t5[NBUCKET:NBUCKET + 1, :], 1.0).then_inc(ones_set, 1)
            for t in range(TT):
                mean_square(0, t)
            for t in range(TT):
                for h in range(2):
                    normalise(0, t, h)
            dve.wait_ge(scale_in, 16)
            dve.wait_ge(raw_in[0], 16)
            w = raw[:, 0, :].rearrange("p (g k n) -> p g k n", g=4, k=2)
            scale = pt[:, 0:2, :].rearrange("p a (g n) -> p (a g) n", g=2).unsqueeze(2).broadcast_to([P, 4, 2, FB])
            dve.tensor_tensor(w, w, scale, ALU.mult).then_inc(pool_scaled, 1)
            for k in range(4):
                if k == 1:
                    split(0)
                dve.wait_ge(hT_hi, k + 1)
                dve.tensor_tensor(h_lo[:, 2 * k:2 * k + 2, :], bank[k][:, :].rearrange("p (c k) -> p c k", c=2),
                                  h_hi[:, 2 * k:2 * k + 2, :].bitcast(F32), ALU.subtract).then_inc(hT_lo, 1)
            split(1)
            ffn(0)

            for ev in moba_script():
                k = ev[0]
                if k == "q_norm":
                    norm(2)
                    split(MOBA_U + 1)
                elif k == "kv_norm":
                    for t in range(TT):
                        for h in range(2):
                            normalise(3, t, h)
                elif k == "kv_h":
                    for t in range(TT):
                        for h in range(2):
                            h_lo_out(3, t, h)
                elif k == "split" and ev[1] < 17:
                    split(MOBA_U + ev[1])
                elif k == "S":
                    i = ev[1]
                    if i == 0:
                        dve.wait_ge(bias_in, 16)
                    maxima(i, [down_from(bias_moba[:, i, :], P - 1, P), down_from(bias_moba[:, i, :], T - 1, T)], P)
                elif k == "N":
                    normal(ev[1], P)
                elif k == "O":
                    g = ev[1]
                    o_low(g, 0 if g == 3 else 6 + g % 2, 2 * g)
            ffn(1)

            def final_norm_1():
                for t in range(TT):
                    for h in range(2):
                        add_residual(4, t, h)
                    mean_square(4, t)
                    for h in range(2):
                        normalise(5, t, h)
                    if t:
                        for h in range(2):
                            h_lo_out(6, 0, h)
                    mean_square(5, t)
                    for h in range(2):
                        normalise(6, t, h)
                for h in range(2):
                    h_lo_out(6, 1, h)

            def mix(l):
                i0, q0, p0 = stage_items(l)
                u0 = MIX_U[l]
                if l == 0:
                    final_norm_1()
                else:
                    norm(8)
                split(u0 + 1)
                for ev in mix_script():
                    k = ev[0]
                    if k == "split" and ev[1] < 16:
                        split(u0 + ev[1])
                    elif k == "proj" and ev[1] == 1:
                        dve.wait_ge(mla_sq, 3 * l + 2)
                        dve.tensor_scalar(msq[:, 2:4], msm[:, 0:2], EPS, None, ALU.add).then_inc(mla_ms, 1)
                        dve.wait_ge(mla_rs, l + 1)
                        for t in range(TT):
                            e = dve.tensor_scalar(latq(t), bank[4][:, t * T:(t + 1) * T], rstd[:, 2 + t:3 + t], None, ALU.mult)
                        e.then_inc(mla_lat, 1)
                        dve.wait_ge(mla_sq, 3 * l + 3)
                        for r in range(2):
                            rr = slice(64 + 32 * r, 96 + 32 * r)
                            e = dve.tensor_tensor(ropet[64:96, r, 0:T], bank[5][rr, T:2 * T], rope[rr, 1, :], ALU.mult)
                        e.then_inc(mla_rope, 1)
                        dve.wait_ge(mla_rope, 4 * l + 1)
                        if l:
                            dve.wait_ge(scores, i0 - 16)
                        dve.tensor_tensor(qall[64:96, 4:8, :], ropet[64:96, 0, 0:T].unsqueeze(1).broadcast_to([32, 4, T]),
                                          ropet[64:96, 1, 0:T].unsqueeze(1).broadcast_to([32, 4, T]), ALU.add).then_inc(mla_rope, 1)
                    elif k == "mla_T":
                        dve.wait_ge(kv_sum, l + 1)
                        dve.tensor_scalar(msq[:, 4:6], bank[1][:, 0:TT], EPS, None, ALU.add).then_inc(kv_mean, 1)
                    elif k == "mla_B":
                        dve.wait_ge(kv_bcast, l + 1)
                        then_wait(dve.tensor_copy(latT[:, 2, :], bank[3][:, 0:T]))
                        dve.scalar_tensor_tensor(out=latT[:, 2, :], in0=bank[5][:, 0:T], scalar=mlag[:, l, 2:3], in1=latT[:, 2, :],
                                                 op0=ALU.mult, op1=ALU.mult).then_inc(kv_lat, 1)
                    elif k == "mla_G":
                        dve.wait_ge(mla_g, 3 * l + 1)
                        dve.wait_ge(mla_rope, 4 * l + 2)
                        for c2 in range(2):
                            for r in range(2):
                                rr = slice(64 + 32 * r, 96 + 32 * r)
                                e = dve.tensor_tensor(ropet[64:96, r, :].rearrange("p (c k) -> p c k", c=2),
                                                      bank[c2][rr, :].rearrange("p (c k) -> p c k", c=2),
                                                      rope[rr, 0, :].unsqueeze(1).broadcast_to([32, 2, T]), ALU.mult)
                            then_wait(e)
                            e = dve.tensor_tensor(qall[64:96, 2 * c2:2 * c2 + 2, :],
                                                  ropet[64:96, 0, :].rearrange("p (c k) -> p c k", c=2),
                                                  ropet[64:96, 1, :].rearrange("p (c k) -> p c k", c=2), ALU.add)
                            e.then_inc(mla_rope, 1)
                            dve.wait_ge(mla_rope, 4 * l + 3 + c2)
                    elif k == "S":
                        i = ev[1]
                        if i < 4:
                            b = None
                        elif i < 8:
                            if i == 4:
                                dve.wait_ge(na_ready, 8 * (l + 1))
                            b = [down_from(bias_na[:, q, i - 4, :], T - 1, T) for q in range(2)]
                        else:
                            if i == 8:
                                dve.wait_ge(bias2_in, 32)
                            t5 = bias_diff[:, (i - 8) // 2, :] if i < 16 else bias_dil[:, i - 16, :]
                            b = [down_from(t5, T - 1, T), down_from(t5, T + P - 1, T)]
                        maxima(i0 + i, b)
                    elif k == "N":
                        i = ev[1]
                        second = 8 <= i < 16 and i % 2
                        normal(i0 + i, T, neglam[:, l:l + 1] if second else None)
                    elif k == "diff_stats":
                        dve.wait_ge(d_sq, l + 1)
                        dve.tensor_reduce(dsq[:, :], dsquare.rearrange("p (g n) -> p g n", n=HD), AX_X, ALU.add).then_inc(d_red, 1)
                        dve.wait_ge(d_red, l + 1)
                        dve.tensor_scalar(dms[:, :], dsq[:, :], EPS, None, ALU.add).then_inc(d_ms, 1)
                    elif k == "diff_norm":
                        dve.wait_ge(d_rs, l + 1)
                        dve.tensor_tensor(dno.rearrange("p (g n) -> p g n", n=HD), bank[6][:, :].rearrange("p (g n) -> p g n", n=HD),
                                          drs[:, :].unsqueeze(2).broadcast_to([P, 8, HD]), ALU.mult).then_inc(d_n, 1)
                    elif k == "diff_T":
                        q = q0 + T_DIFF
                        dve.wait_ge(pt_ready, q + 1)
                        dve.scalar_tensor_tensor(out=o_lo[:, 2:4, :].rearrange("p a b -> p (a b)"), in0=bank[2 + q % 2][:, :],
                                                 scalar=subln_s[:, l:l + 1],
                                                 in1=o_hi[:, 2:4, :].bitcast(F32).rearrange("p a b -> p (a b)"),
                                                 op0=ALU.mult, op1=ALU.subtract).then_inc(out_lo, 1)
                    elif k == "O":
                        g = ev[1]
                        o_low(OUT_HI[l][g], [6, 7, None, 0][g], MIX_OUT_CHUNK[g])

            mix(0)
            ffn(2)
            mix(1)
            ffn(3)
            for t in range(TT):
                for h in range(2):
                    add_residual(9, t, h)
                mean_square(9, t)
                for h in range(2):
                    normalise(10, t, h)

        @block.tensor
        def _(pe):
            def three(dst, ahi, alo, bhi, blo, first, last):
                pe.matmul(dst, ahi, bhi, start=first, stop=False)
                pe.matmul(dst, ahi, blo, start=False, stop=False)
                return pe.matmul(dst, alo, bhi, start=False, stop=last)

            def w8(n, width=FB):
                s = slot_of(n)
                return tuple(w[:, s, 0:KC * width].rearrange("p (k n) -> p k n", k=KC) for w in (whi, wlo))

            def w2(n):
                s = slot_of(n)
                return tuple(w[:, s, :].rearrange("p (k n) -> p k n", k=2) for w in (whi, wlo))

            def feature_major(n, bk, toks, j, src):
                hi, lo = w8(n)
                for kc in range(KC):
                    mm = three(bank[bk][:, j * T + toks.start:j * T + toks.stop],
                               hi[:, kc, j * P:(j + 1) * P], lo[:, kc, j * P:(j + 1) * P],
                               src[0][:, kc, toks], src[1][:, kc, toks], kc == 0, kc == KC - 1)
                return mm

            def first_feature_major(n, bk, src, j):
                hi, lo = w8(n)
                pe.wait_ge(lo_ready, n + 1)
                for kc in range(KC):
                    if kc % 4 == 0:
                        pe.wait_ge(hT_hi, 4 * HT_NO[j] + 3 + kc // 4)
                    for w in (hi, lo):
                        pe.matmul(bank[bk][:, 0:T], w[:, kc, 0:P], src[0][:, kc, :], start=(kc == 0 and w is hi), stop=False)
                wait_h(j, 1)
                for kc in range(KC):
                    pe.matmul(bank[bk][:, 0:T], hi[:, kc, 0:P], src[1][:, kc, :], start=False, stop=(kc == KC - 1))
                return feature_major(n, bk, ALL, 1, src)

            def first_token_major(n, bk, t, j):
                hi, lo = w8(n)
                pe.wait_ge(lo_ready, n + 1)
                dst = bank[bk][:, t * FB:(t + 1) * FB]
                for kc in range(KC):
                    if kc % 4 == 0:
                        pe.wait_ge(hT_hi, 4 * HT_NO[j] + 2 * t + kc // 4 + 1)
                    pe.matmul(dst, h_hi[:, kc, t * P:(t + 1) * P], hi[:, kc, :], start=(kc == 0), stop=False)
                    pe.matmul(dst, h_hi[:, kc, t * P:(t + 1) * P], lo[:, kc, :], start=False, stop=False)
                wait_h(j, t)
                for kc in range(KC):
                    mm = pe.matmul(dst, h_lo[:, kc, t * P:(t + 1) * P], hi[:, kc, :], start=False, stop=(kc == KC - 1))
                return mm

            def token_major(n, bk, col, width, t, src, wcols, total=FB):
                hi, lo = w8(n, total)
                for kc in range(KC):
                    mm = three(bank[bk][:, col:col + width], src[0][:, kc, t * P:(t + 1) * P], src[1][:, kc, t * P:(t + 1) * P],
                               hi[:, kc, wcols], lo[:, kc, wcols], kc == 0, kc == KC - 1)
                return mm

            def residual(n, chunks, src, first, last, tiles=range(TT), before_last=None):
                hi, lo = w2(n)
                for t in tiles:
                    for h in range(2):
                        if before_last is not None and h:
                            transposes(before_last, 0)
                        for k in range(2):
                            mm = three(bank[ACC[2 * t + h]][:, :], src[0][:, chunks + k, t * P:(t + 1) * P],
                                       src[1][:, chunks + k, t * P:(t + 1) * P], hi[:, k, h * HALF:(h + 1) * HALF],
                                       lo[:, k, h * HALF:(h + 1) * HALF], first and k == 0, last and k == 1)
                        if last and (t, h) != (1, 1):
                            mm.then_inc(acc_ready, 1)
                return mm

            def used(bump):
                bump.then_inc(units_used, 1)

            def transposes(j, t):
                for h in range(2):
                    pe.wait_ge(xn_ready, 4 * XN_NO[j] + 2 * t + h + 1)
                    if HT_NO[j] == 3:
                        pe.wait_ge(hT_lo, 4 * 2 + 2 * t + h + 1)
                    for k in range(4):
                        mm = pe.transpose(bank[2 * t + h][:, k * P:(k + 1) * P],
                                          xn[:, t, (4 * h + k) * P:(4 * h + k + 1) * P], ident[:, :])
                    mm.then_inc(xT_ready, 1)

            H = (h_hi, h_lo)
            O = (o_hi, o_lo)
            ALL = slice(0, T)

            def tile(t):
                return slice(t * P, (t + 1) * P)

            def wait_h(j, t):
                pe.wait_ge(hT_lo, 4 * HT_NO[j] + 2 * t + 2)

            pe.wait_ge(ones_set, 2)
            pe.wait_ge(table_in, 32)
            pe.wait_ge(onehot_in, 48)
            K = NBUCKET + 1
            for i, lhs in enumerate((tab_moba[0:K, :], tab_t5[0:K, 0:4], tab_t5[0:K, 4:8])):
                pe.matmul(bank[4 + i][0:lhs.shape[1], :], lhs, onehots[0:K, i, :], start=True, stop=True).then_inc(vec_done, 1)

            pe.wait_ge(band_in, 16)
            pe.wait_ge(xn_ready, 4)
            for g in range(4):
                for k in range(2):
                    for s in range(TT):
                        mm = pe.matmul(bank[g][:, k * T + s * P:(k + 1) * T], xn[:, s, g * 256 + k * P:g * 256 + (k + 1) * P],
                                       band[:, g, s, s * P:], start=(s == 0), stop=(s == TT - 1))
                mm.then_inc(pool_d, 1)
            pe.wait_ge(lo_ready, 1)
            pe.wait_ge(vec_out, 3)
            hi, lo = w8(POOL_U)
            for t in range(TT):
                for h in range(2):
                    for g in (2 * h, 2 * h + 1):
                        pe.wait_ge(hT_lo, g + 1)
                        for k in range(2):
                            mm = three(bank[ACC[2 * t + h]][:, (g % 2) * 256:(g % 2) * 256 + 256],
                                       h_hi[:, 2 * g + k, tile(t)], h_lo[:, 2 * g + k, tile(t)],
                                       hi[:, 2 * g + k, :], lo[:, 2 * g + k, :], k == 0, k == 1)
                    if (t, h) != (1, 1):
                        mm.then_inc(acc_ready, 1)
            used(mm)

            def ffn(f):
                u0, e0 = FFN_U[f], NB * f
                j = [1, 4, 7, 9][f]
                if f == 0:
                    pe.wait_ge(small_in, 15 * 16)
                for t in range(TT):
                    transposes(j, t)
                used(first_feature_major(u0, ACC[0], H, j))
                pe.wait_ge(lo_ready, u0 + 2)
                for jj in range(2):
                    mm = feature_major(u0 + 1, ACC[1], ALL, jj, H)
                used(mm)

                def gate_up(b, par, off):
                    for u in range(2):
                        pe.wait_ge(lo_ready, u0 + 3 * b + u)
                        if off >= 2:
                            pe.wait_ge(glu_ready, e0 + b - 1)
                        for jj in range(2):
                            mm = feature_major(u0 - 1 + u, 2 * par + u, ALL, jj, H)
                        used(mm)

                def down(b, par, k, first=False, last=False):
                    pe.wait_ge(act_ready, e0 + b + 1)
                    pe.wait_ge(lo_ready, k + 1)
                    used_slot = (u0 + 1) if not last else (u0 + 3 * NB - 1)
                    return residual(used_slot, 2 * par, O, first, last)

                gate_up(1, 1, 1)
                used(down(0, 0, u0 + 4, first=True))
                with pe.Fori(2, NB - 1, 2) as b:
                    gate_up(b, 0, 2)
                    used(down(b - 1, 1, u0 + 1 + 3 * b))
                    gate_up(b + 1, 1, 2)
                    used(down(b, 0, u0 + 4 + 3 * b))
                b = NB - 1
                gate_up(b, 0, 2)
                for t in range(TT):
                    pe.wait_ge(act_ready, e0 + b + t)
                    pe.wait_ge(lo_ready, u0 + 2 + 3 * b + t)
                    mm = residual(u0 + 1 + 3 * b, 2, O, False, False, (t,))
                    if t:
                        used(mm)
                    if t == 0:
                        pe.wait_ge(act_ready, e0 + b + 1)
                        pe.wait_ge(lo_ready, u0 + 3 + 3 * b)
                    mm = residual(u0 + 2 + 3 * b, 0, O, False, True, (t,), {0: 2, 2: 8}.get(f) if t else None)
                used(mm)

            ffn(0)

            def scores_of(i, q, k, causal):
                if i >= 2:
                    pe.wait_ge(exped, i - 1)
                for qt in range(2):
                    w = P if causal and qt == 0 else T
                    mm = pe.matmul(bank[i % 2][:, qt * T:qt * T + w], q[:, qt * P:(qt + 1) * P], k[:, 0:w], start=True, stop=True)
                mm.then_inc(scores, 1)

            def transpose_head(q, i, causal):
                if q >= 2:
                    pe.wait_ge(pt_ready, q - 1)
                at = 0
                for kt in range(2):
                    for qt in range(2):
                        if causal and kt > qt:
                            continue
                        mm = pe.transpose(bank[2 + q % 2][:, at:at + P], pr[:, i % 8, qt, kt * P:(kt + 1) * P], ident[:, :])
                        at += P
                mm.then_inc(transposed, 1)

            def head_out(head, q, h, bk, v, causal):
                pe.wait_ge(pt_ready, q + 1)
                rows = slice((h % 2) * HD, (h % 2) * HD + HD)
                c0 = (h // 2) * T
                p = pt[:, head % 4, :]
                pe.matmul(bank[bk][rows, c0:c0 + T], v[:, 0, h * HD:(h + 1) * HD], p[:, 0:T], start=True, stop=False)
                if causal:
                    mm = pe.matmul(bank[bk][rows, c0 + P:c0 + T], v[:, 1, h * HD:(h + 1) * HD], p[:, T:T + P], start=False, stop=True)
                else:
                    mm = pe.matmul(bank[bk][rows, c0:c0 + T], v[:, 1, h * HD:(h + 1) * HD], p[:, T:2 * T], start=False, stop=True)
                mm.then_inc(pv_done, 1)

            for ev in moba_script():
                k = ev[0]
                if k == "q_norm":
                    transposes(2, 1)
                elif k == "kv_h":
                    for t in range(TT):
                        transposes(3, t)
                elif k == "unit":
                    n = ev[1]
                    u = MOBA_U + n
                    pe.wait_ge(lo_ready, u + 1)
                    if n < 12:
                        if n >= 2:
                            pe.wait_ge(proj_out, n - 1)
                        if n == 4:
                            wait_h(3, 1)
                        if n == 0:
                            mm = first_feature_major(u, 4, O, 2)
                        for x2 in range(2 if n else 0):
                            if n < 4:
                                mm = feature_major(u, 4 + n % 2, ALL, x2, O)
                            elif n % 2 == 0:
                                mm = feature_major(u, 4 + n % 2, ALL, x2, H)
                            else:
                                mm = token_major(u, 4 + n % 2, x2 * FB, FB, x2, H, slice(0, FB))
                        used(mm)
                    else:
                        if n == 12:
                            pe.wait_ge(proj_out, 12)
                        pe.wait_ge(out_lo, 3 if n == 12 else n - 11)
                        mm = residual(u, 2 * (n - 12), O, n == 12, n == 15)
                        used(mm)
                elif k == "S":
                    i = ev[1]
                    g, h = i // 4, i % 4
                    rows = slice((h % 2) * HD, (h % 2) * HD + HD)
                    pe.wait_ge(proj_out, 5 + 2 * g)
                    scores_of(i, qall[rows, 2 * g + h // 2, :], kg[rows, g % 2, h // 2, :], True)
                elif k == "T":
                    pe.wait_ge(normed, ev[1] + 1)
                    transpose_head(ev[1], ev[1], True)
                elif k == "V":
                    i = ev[1]
                    g = i // 4
                    if i % 4 == 0:
                        pe.wait_ge(proj_out, 6 + 2 * g)
                        if g == 2:
                            pe.wait_ge(out_lo, 1)
                        if g == 3:
                            pe.wait_ge(exped, 16)
                    head_out(i, i, i % 4, 0 if g == 3 else 6 + g % 2, vg[:, g % 2], True)
            ffn(1)

            def mix(l):
                i0, q0, p0 = stage_items(l)
                hd0 = 16 + 16 * l
                u0 = MIX_U[l]
                j = 6 + 2 * l
                if l == 0:
                    transposes(6, 0)
                nt = 0
                t_of = {}
                for ev in mix_script():
                    k = ev[0]
                    if k == "unit":
                        n = ev[1]
                        u = u0 + n
                        bk = mix_bank(n)
                        if n:
                            pe.wait_ge(lo_ready, u + 1)
                        if 4 <= n < 11:
                            pe.wait_ge(proj_out, p0 + n - 3)
                        if n == 1:
                            hi, lo = w8(u, 192)
                            for kc in range(KC):
                                three(bank[bk][:, 0:T], hi[:, kc, 0:P], lo[:, kc, 0:P],
                                      h_hi[:, kc, :], h_lo[:, kc, :], kc == 0, kc == KC - 1)
                            for kc in range(KC):
                                mm = three(bank[bk][:, T:2 * T], hi[:, kc, 64:192], lo[:, kc, 64:192],
                                           h_hi[:, kc, :], h_lo[:, kc, :], kc == 0, kc == KC - 1)
                            used(mm)
                        elif n == 0:
                            first_token_major(u, bk, 0, j)
                            transposes(j, 1)
                            used(first_token_major(u, bk, 1, j))
                        elif n < 11 and (n - 2) % 3 == 2:
                            for t in range(TT):
                                mm = token_major(u, bk, t * FB, FB, t, H, slice(0, FB))
                            used(mm)
                        elif n < 11:
                            for x2 in range(2):
                                mm = feature_major(u, bk, ALL, x2, H)
                            used(mm)
                        else:
                            if n == 11:
                                pe.wait_ge(proj_out, p0 + 9)
                                pe.wait_ge(d_n, l + 1)
                                pe.wait_ge(out_lo, OUT_LO[l][1] + 1)
                            else:
                                pe.wait_ge(out_lo, OUT_LO[l][n - 11] + 1)
                            mm = residual(u, MIX_OUT_CHUNK[n - 11], O, n == 11, n == 14)
                            used(mm)
                    elif k == "mla_T":
                        pe.wait_ge(mla_sq, 3 * l + 3)
                        pe.wait_ge(consts_set, 2)
                        for t in range(TT):
                            mm = pe.matmul(bank[1][:, t:t + 1], kv_sq[:, tile(t)], ones[:, :], start=True, stop=True)
                        mm.then_inc(kv_sum, 1)
                        pe.wait_ge(mla_lat, l + 1)
                        for cc in range(2):
                            for t in range(TT):
                                mm = pe.transpose(bank[0][:, cc * T + t * P:cc * T + (t + 1) * P],
                                                  latq(t)[:, cc * P:(cc + 1) * P], ident[:, :])
                        mm.then_inc(mla_t, 1)
                    elif k == "mla_B":
                        pe.wait_ge(kv_rsqrt, l + 1)
                        for t in range(TT):
                            mm = pe.matmul(bank[3][:, t * P:(t + 1) * P], rstd[:, 4 + t:5 + t].broadcast_to([P, P]), ident[:, :],
                                           start=True, stop=True)
                        mm.then_inc(kv_bcast, 1)
                    elif k == "mla_G":
                        pe.wait_ge(mla_tT, l + 1)
                        pe.wait_ge(layer_in[l], 16 * 7)
                        for h in range(4):
                            for kc in range(2):
                                mm = pe.matmul(bank[h // 2][:, (h % 2) * T:(h % 2 + 1) * T], wuq[:, kc, h, :], latT[:, kc, :],
                                               start=(kc == 0), stop=(kc == 1))
                        mm.then_inc(mla_g, 1)
                        pe.wait_ge(kv_lat, l + 1)
                        for h in range(4):
                            mm = pe.matmul(bank[2 + h // 2][0:HD, (h % 2) * T:(h % 2 + 1) * T], wukv[:, h, 0, :], latT[:, 2, :],
                                           start=True, stop=True)
                        mm.then_inc(mla_g, 1)
                        pe.wait_ge(proj_out, p0 + 1)
                        for t in range(TT):
                            mm = pe.matmul(bank[6][:, t * T:(t + 1) * T], latT[:, 2, tile(t)], wukv[:, :, 1, :], start=True, stop=True)
                        mm.then_inc(mla_g, 1)
                    elif k == "S":
                        i = ev[1]
                        if i == 0:
                            pe.wait_ge(mla_copied, l + 1)
                            pe.wait_ge(mla_rope, 4 * l + 4)
                        if i < 4:
                            q, kk = qall[0:MLA_D, i, :], qall[0:MLA_D, 4 + i, :]
                        else:
                            g = 0 if i < 8 else 1 if i < 16 else 2
                            pe.wait_ge(proj_out, p0 + 3 * g + 2)
                            par = (g + 1) % 2
                            if g == 1:
                                h, comp = (i - 8) // 2, i % 2
                                rows = slice((h % 2) * HD + comp * 32, (h % 2) * HD + comp * 32 + 32)
                            else:
                                h = i % 4
                                rows = slice((h % 2) * HD, (h % 2) * HD + HD)
                            q, kk = qg[rows, par, h // 2, :], kg[rows, par, h // 2, :]
                        scores_of(i0 + i, q, kk, False)
                    elif k == "T":
                        h = ev[1]
                        item = h if h < 8 else 8 + 2 * (h - 8) if h < 12 else h + 4
                        pe.wait_ge(normed, i0 + item + (2 if 8 <= h < 12 else 1))
                        if nt == T_DIFF + 2:
                            pe.wait_ge(out_lo, OUT_LO[l][2] + 1)
                        transpose_head(q0 + nt, i0 + item, False)
                        t_of[h] = q0 + nt
                        nt += 1
                    elif k == "V":
                        h = ev[1]
                        g = h // 4
                        par = g % 2
                        if h % 4 == 0:
                            if g:
                                pe.wait_ge(proj_out, p0 + 3 * (g - 1) + 3)
                            if g == 2:
                                pe.wait_ge(out_lo, OUT_LO[l][0] + 1)
                            if g == 3:
                                pe.wait_ge(exped, i0 + 20)
                        if g == 2:
                            pe.wait_ge(pt_ready, t_of[h] + 1)
                            p = pt[:, (hd0 + h) % 4, :]
                            for qt in range(2):
                                for kt in range(2):
                                    mm = pe.matmul(bank[6][:, qt * T + (h % 4) * HD:qt * T + (h % 4 + 1) * HD],
                                                   p[:, kt * T + qt * P:kt * T + (qt + 1) * P],
                                                   vg[:, par, kt, (h % 4) * HD:(h % 4 + 1) * HD], start=(kt == 0), stop=(kt == 1))
                            mm.then_inc(pv_done, 1)
                        else:
                            head_out(hd0 + h, t_of[h], h % 4, [6, 7, None, 0][g], vg[:, par], False)
                    elif k == "diff_T":
                        pe.wait_ge(d_n, l + 1)
                        q = q0 + nt
                        pe.wait_ge(pt_ready, q - 1)
                        for cc in range(2):
                            for qt in range(2):
                                mm = pe.transpose(bank[2 + q % 2][:, cc * T + qt * P:cc * T + (qt + 1) * P],
                                                  dno[:, qt * T + cc * P:qt * T + (cc + 1) * P], ident[:, :])
                        mm.then_inc(transposed, 1)
                        nt += 1

            mix(0)
            ffn(2)
            mix(1)
            ffn(3)


_INS = ["x", "norm_mixer", "norm_ffn", "pool_w", "pool_scale", "kv_norm", "w_kv", "w_q", "w_o", "rel_bias",
        "w_gate_up", "w_down", "final_norm", "attn_norm_2", "w_in_2", "na_rpb_2", "diff_lambda_2",
        "diff_subln_2", "mla_q_norm_2", "w_uq_2", "mla_kv_norm_2", "w_ukv_2", "t5_table_2", "w_o_2",
        "ffn_norm_2", "w_gate_2", "w_up_2", "w_down_2", "final_norm_2"]


def kernel(**inputs):
    import concourse.bacc as bacc
    from concourse.bass_utils import run_bass_kernel_spmd

    nc = bacc.Bacc("TRN2", target_bir_lowering=False, num_devices=1)
    arrays, a, c = {}, {}, {}
    for name in _INS:
        v = np.asarray(inputs[name])
        if name == "na_rpb_2":
            v = v[:, :, ::-1, ::-1]
        v = np.ascontiguousarray(v)
        arrays["in_" + name] = v
        a[name] = nc.dram_tensor("in_" + name, v.shape, F32, kind="ExternalInput").ap()
    for name, v in shape_constants().items():
        v = np.ascontiguousarray(v)
        arrays["in_" + name] = v
        c[name] = nc.dram_tensor("in_" + name, v.shape, F32, kind="ExternalInput").ap()
    out = nc.dram_tensor("result", (1, T, D), F32, kind="ExternalOutput").ap()
    bass_two_stacks(nc, a, c, out)
    r = run_bass_kernel_spmd(nc, [arrays], core_ids=[0])
    return r.results[0]["result"]
```
